# Optimizing a Trainium2 kernel written in Bass

```python
import jax
import jax.numpy as jnp
from jax import lax
import numpy as np

D_MODEL = 1024
BATCH = 1
SEQ = 256
DEPTH = 2

N_BRANCH = 3
W_BRANCH = 1024
SC_KERNEL = 3
CV_KERNEL = 31
CHUNK = 128
SG_HEADS = 8
SG_HEAD_DIM = W_BRANCH // SG_HEADS
IN_COLS = 7 * W_BRANCH
N_EXPERTS = 16
N_GROUPS = 4
EXPERTS_PER_GROUP = N_EXPERTS // N_GROUPS
TOP_K = 2
D_EXPERT = 512
MOE_BLOCK = 128
ALPHA = (2.0 * DEPTH) ** 0.25
BETA = (8.0 * DEPTH) ** -0.25
LN_EPS = 1e-5

kernel_name = 'hybrid_conv_sgu_moe_deepnorm'

def layer_norm(x, g, b):
    xf = x.astype(jnp.float32)
    mu = jnp.mean(xf, axis=-1, keepdims=True)
    xc = xf - mu
    var = jnp.mean(xc * xc, axis=-1, keepdims=True)
    y = xc * lax.rsqrt(var + LN_EPS) * g.astype(jnp.float32) + b.astype(jnp.float32)
    return y.astype(x.dtype)

def causal_depthwise_conv(x, w):
    k = w.shape[0]
    return lax.conv_general_dilated(
        x, w[:, None, :], window_strides=(1,), padding=[(k - 1, 0)],
        dimension_numbers=('NWC', 'WIO', 'NWC'), feature_group_count=x.shape[-1])

def token_mixer(u, w_in, sc_conv, cv_conv, cv_conv_b, cv_ln_g, cv_ln_b, sg_ln_g, sg_ln_b,
                sg_w, sg_b, w_branch, w_gate, b_gate, w_o):
    bsz, seq, _ = u.shape
    proj = jnp.einsum('bsd,dn->bsn', u, w_in)
    wb = W_BRANCH
    sc_b, sc_c, sc_h, cv_a, cv_g, sg_u, sg_v = jnp.split(
        proj, [wb, 2 * wb, 3 * wb, 4 * wb, 5 * wb, 6 * wb], axis=-1)
    y_a = sc_b * causal_depthwise_conv(sc_c * sc_h, sc_conv)
    cv = cv_a * jax.nn.sigmoid(cv_g)
    cv = causal_depthwise_conv(cv, cv_conv) + cv_conv_b
    y_b = jax.nn.silu(layer_norm(cv, cv_ln_g, cv_ln_b))
    sg_u = jax.nn.gelu(sg_u)
    sg_v = layer_norm(jax.nn.gelu(sg_v), sg_ln_g, sg_ln_b)
    v = sg_v.reshape(bsz, seq // CHUNK, CHUNK, SG_HEADS, SG_HEAD_DIM)
    mask = jnp.tril(jnp.ones((CHUNK, CHUNK), dtype=sg_w.dtype))
    v = jnp.einsum('hts,bnshc->bnthc', sg_w * mask, v) + sg_b.T[:, :, None]
    y_c = sg_u * v.reshape(bsz, seq, W_BRANCH)
    branches = jnp.stack([y_a, y_b, y_c], axis=0)
    y = jnp.einsum('nbsw,nwd->nbsd', branches, w_branch)
    gates = jax.nn.sigmoid(jnp.einsum('bsd,dne->nbse', u, w_gate) + b_gate[:, None, None, :])
    merged = jnp.sum(gates * y, axis=0)
    return jnp.einsum('bsd,de->bse', merged, w_o)

def grouped_moe(u, w_router, b_router, w1, w3, w2):
    bsz, seq, d = u.shape
    n_tok = bsz * seq
    xt = u.reshape(n_tok, d)
    logits = jnp.einsum('td,de->te', xt, w_router).astype(jnp.float32)
    scores = jax.nn.softmax(logits, axis=-1)
    sel = (scores + b_router.astype(jnp.float32)).reshape(n_tok, N_GROUPS, EXPERTS_PER_GROUP)
    group_score = jnp.sum(lax.top_k(sel, TOP_K)[0], axis=-1)
    g_idx = jnp.argmax(group_score, axis=-1).astype(jnp.int32)
    sel_in = jnp.take_along_axis(sel, g_idx[:, None, None], axis=1)[:, 0]
    _, loc = lax.top_k(sel_in, TOP_K)
    eid = g_idx[:, None] * EXPERTS_PER_GROUP + loc.astype(jnp.int32)
    gate = jnp.take_along_axis(scores, eid, axis=1)
    gate = gate / jnp.sum(gate, axis=-1, keepdims=True)
    n_assign = n_tok * TOP_K
    e_flat = eid.reshape(n_assign)
    tok_flat = jnp.arange(n_assign, dtype=jnp.int32) // TOP_K
    order = jnp.argsort(e_flat)
    e_sorted = e_flat[order]
    tok_sorted = tok_flat[order]
    gate_sorted = gate.reshape(n_assign)[order]
    counts = jnp.zeros((N_EXPERTS,), jnp.int32).at[e_flat].add(1)
    padded = (counts + MOE_BLOCK - 1) // MOE_BLOCK * MOE_BLOCK
    pad_end = jnp.cumsum(padded)
    pad_start = pad_end - padded
    seg_start = jnp.cumsum(counts) - counts
    dest = pad_start[e_sorted] + jnp.arange(n_assign, dtype=jnp.int32) - seg_start[e_sorted]
    n_blocks = (n_assign + N_EXPERTS * (MOE_BLOCK - 1) + MOE_BLOCK - 1) // MOE_BLOCK
    buf = jnp.zeros((n_blocks * MOE_BLOCK, d), u.dtype).at[dest].set(xt[tok_sorted])
    block_start = jnp.arange(n_blocks, dtype=jnp.int32) * MOE_BLOCK
    block_e = jnp.minimum(jnp.searchsorted(pad_end, block_start, side='right'),
                          N_EXPERTS - 1).astype(jnp.int32)

    def expert_block(args):
        xb, e = args
        h = jax.nn.silu(xb @ w1[e]) * (xb @ w3[e])
        return h @ w2[e]

    out_buf = lax.map(expert_block, (buf.reshape(n_blocks, MOE_BLOCK, d), block_e))
    out_buf = out_buf.reshape(n_blocks * MOE_BLOCK, d)
    contrib = out_buf[dest] * gate_sorted.astype(u.dtype)[:, None]
    out = jnp.zeros((n_tok, d), u.dtype).at[tok_sorted].add(contrib)
    return out.reshape(bsz, seq, d)

def setup_inputs(seed: int = 0) -> dict:
    key = jax.random.key(seed)
    ks = jax.random.split(key, 32)
    f32 = jnp.float32

    def nrm(k, shape, s):
        return jax.random.normal(k, shape, f32) * s

    d, wb, e, fe = D_MODEL, W_BRANCH, N_EXPERTS, D_EXPERT
    return {
        'x': nrm(ks[0], (BATCH, SEQ, d), 1.0),
        'c': nrm(ks[1], (BATCH, d), 1.0),
        'w_ada': nrm(ks[2], (DEPTH, d, 6 * d), d ** -0.5),
        'b_ada': nrm(ks[3], (DEPTH, 6 * d), 0.02),
        'w_in': nrm(ks[4], (DEPTH, d, IN_COLS), d ** -0.5),
        'sc_conv': nrm(ks[5], (DEPTH, SC_KERNEL, wb), SC_KERNEL ** -0.5),
        'cv_conv': nrm(ks[6], (DEPTH, CV_KERNEL, wb), CV_KERNEL ** -0.5),
        'cv_conv_b': nrm(ks[7], (DEPTH, wb), 0.02),
        'cv_ln_g': 1.0 + nrm(ks[8], (DEPTH, wb), 0.05),
        'cv_ln_b': nrm(ks[9], (DEPTH, wb), 0.02),
        'sg_ln_g': 1.0 + nrm(ks[10], (DEPTH, wb), 0.05),
        'sg_ln_b': nrm(ks[11], (DEPTH, wb), 0.02),
        'sg_w': nrm(ks[12], (DEPTH, SG_HEADS, CHUNK, CHUNK), CHUNK ** -0.5),
        'sg_b': 1.0 + nrm(ks[13], (DEPTH, SG_HEADS, CHUNK), 0.1),
        'w_branch': nrm(ks[14], (DEPTH, N_BRANCH, wb, d), BETA * wb ** -0.5),
        'w_gate': nrm(ks[15], (DEPTH, d, N_BRANCH, d), d ** -0.5),
        'b_gate': nrm(ks[16], (DEPTH, N_BRANCH, d), 0.02),
        'w_o': nrm(ks[17], (DEPTH, d, d), BETA * d ** -0.5),
        'ln1_g': 1.0 + nrm(ks[18], (DEPTH, d), 0.05),
        'ln1_b': nrm(ks[19], (DEPTH, d), 0.02),
        'w_router': nrm(ks[20], (d, e), d ** -0.5),
        'b_router': nrm(ks[21], (e,), 0.01),
        'w1': nrm(ks[22], (DEPTH, e, d, fe), d ** -0.5),
        'w3': nrm(ks[23], (DEPTH, e, d, fe), d ** -0.5),
        'w2': nrm(ks[24], (DEPTH, e, fe, d), BETA * fe ** -0.5),
        'ln2_g': 1.0 + nrm(ks[25], (DEPTH, d), 0.05),
        'ln2_b': nrm(ks[26], (DEPTH, d), 0.02),
    }

def reference(x, c, w_ada, b_ada, w_in, sc_conv, cv_conv, cv_conv_b, cv_ln_g, cv_ln_b,
              sg_ln_g, sg_ln_b, sg_w, sg_b, w_branch, w_gate, b_gate, w_o, ln1_g, ln1_b,
              w_router, b_router, w1, w3, w2, ln2_g, ln2_b):
    c_act = jax.nn.silu(c)
    for l in range(DEPTH):
        mod = jnp.einsum('bd,dn->bn', c_act, w_ada[l]) + b_ada[l]
        shift1, scale1, gate1, shift2, scale2, gate2 = jnp.split(mod[:, None, :], 6, axis=-1)
        u = x * (1.0 + scale1) + shift1
        h = token_mixer(u, w_in[l], sc_conv[l], cv_conv[l], cv_conv_b[l], cv_ln_g[l], cv_ln_b[l],
                        sg_ln_g[l], sg_ln_b[l], sg_w[l], sg_b[l], w_branch[l], w_gate[l],
                        b_gate[l], w_o[l])
        x = layer_norm(ALPHA * x + gate1 * h, ln1_g[l], ln1_b[l])
        u = x * (1.0 + scale2) + shift2
        h = grouped_moe(u, w_router, b_router, w1[l], w3[l], w2[l])
        x = layer_norm(ALPHA * x + gate2 * h, ln2_g[l], ln2_b[l])
    return x


_drawn_inputs = setup_inputs


def setup_inputs(seed=0):
    import zlib

    import numpy as np

    out = dict(_drawn_inputs(seed))
    spreads = {}
    factors = {'cv_conv_b': 8.0,
     'cv_ln_g': 8.0,
     'cv_ln_b': 28.603,
     'sg_ln_g': 8.0,
     'sg_ln_b': 42.584,
     'sg_b': 6.463,
     'b_gate': 8.0}
    for name, (base, spread) in spreads.items():
        noise = np.random.default_rng([zlib.crc32(name.encode()), seed]).standard_normal(out[name].shape)
        drawn = base * np.exp(spread * noise) if base else spread * noise
        out[name] = jnp.asarray(drawn.astype(out[name].dtype))
    for name, factor in factors.items():
        out[name] = (out[name] * factor).astype(out[name].dtype)
    return out
```

```python
from contextlib import ExitStack

import concourse.bass as bass
from concourse import mybir

F32 = mybir.dt.float32
I32 = mybir.dt.int32
ALU = mybir.AluOpType
ACT = mybir.ActivationFunctionType
AX_X = mybir.AxisListType.X

P = 128
DEPTH = 2
D = 1024
T = 256
TT = T // P
KD = D // P
HALF = D // 2
MT = HALF // P
SC_TAPS, CV_TAPS = 3, 31
HEADS = 8
EXPERTS, GROUPS = 16, 4
PER_GROUP = EXPERTS // GROUPS
TOP_K = 2
DE = 512
KE = DE // P
BLOCK = 64
SLOTS = TOP_K * T
ALPHA = (2.0 * DEPTH) ** 0.25
LN_EPS = 1e-5
PRIMED = 1
BIG = 4096.0

RING = 6
SLOT = KD * HALF
BANKS = 8
BANK = 512

SHIFT1, SCALE1, SHIFT2, SCALE2 = 0, 1, 2, 3
SC_W = 4
CV_W = SC_W + SC_TAPS
CV_B = CV_W + CV_TAPS
CV_G, CV_LB = CV_B + 1, CV_B + 2
B_GATE = CV_B + 3
N_CHAN = B_GATE + 3
ROW_SG, ROW_LN1, ROW_LN2, ROW_GATE = 0, 3, 5, 7
N_ROWS = 9
C_ID, C_PREC = 0, P
C_TRI16 = 2 * P
C_IOTA = C_TRI16 + EXPERTS * EXPERTS
N_CONST = C_IOTA + SLOTS

ADA_PARTS = [0, 0, 1, 1, 2, 2, 3, 3, 4, 4, 5, 5]
UNITS = [("ada", 0), ("ada", 1), ("ada", 2), ("ada", 3),
         ("in", 8), ("in", 6), ("in", 9), ("in", 7),
         ("in", 12), ("ada", 4), ("in", 13), ("ada", 5),
         ("in", 2), ("in", 4), ("ada", 6), ("in", 3), ("in", 5), ("ada", 7),
         ("in", 0), ("in", 1), ("ada", 8), ("in", 10), ("in", 11), ("ada", 9),
         ("gate", (0, 0)), ("gate", (0, 1)), ("ada", 10), ("branch", (0, 0)), ("branch", (0, 1)),
         ("ada", 11), ("gate", (2, 0)), ("gate", (2, 1)), ("branch", (2, 0)), ("branch", (2, 1)),
         ("gate", (1, 0)), ("gate", (1, 1)), ("branch", (1, 0)), ("branch", (1, 1)),
         ("o", 0), ("o", 1)]
UNIT = {u: i for i, u in enumerate(UNITS)}
MIX = [len(range(s, len(UNITS), RING)) for s in range(RING)]
MOE_PAIRS = EXPERTS // 2
PER_SLOT = [m + MOE_PAIRS for m in MIX]


def bank_uses():
    uses = [(("ada", i), "dve") for i in range(4)]
    uses += [(("turn1", i), "act" if i % 2 == 0 else "dve") for i in range(KD // 2)]
    drains = {"in": {8: "act", 9: "act", 6: "dve", 7: "dve", 12: "act", 13: "act", 2: "act", 3: "act",
                     4: "dve", 5: "dve", 0: "dve", 1: "dve", 10: "act", 11: "act"}}
    for what, n in UNITS[4:]:
        if (what, n) == ("gate", (0, 0)):
            uses += [(("mix", i), "dve") for i in range(HEADS // 2)]
        if (what, n) == ("gate", (1, 0)):
            uses += [(("mean", 0), "dve"), (("var", 0), "act")]
        if what == "ada":
            uses.append(((what, n), "dve"))
        else:
            who = drains["in"][n] if what == "in" else "act" if what == "gate" else "dve"
            uses += [((what, n, i), who) for i in range(2)]
    uses += [(("turn2", i), "act" if i % 2 == 0 else "dve") for i in range(KD // 2)]
    uses += [(("logits", 0), "dve"), (("ranks", 0), "dve")]
    uses += [(("gather", i), "act" if i % 2 == 0 else "dve") for i in range(KD)]
    return uses


USES = bank_uses()
USE = {what: i for i, (what, _) in enumerate(USES)}
N_USES = len(USES)
N_DRAINED = {e: sum(w == e for _, w in USES) for e in ("act", "dve")}
DRAINED = {what: (e, sum(w == e for _, w in USES[:i + 1])) for i, (what, e) in enumerate(USES)}
DVE_CHAIN = 186


def build(nc, x, c_cols, w_ada, w_in, w_gate, w_branch, w_o, w1, w3, w2, w_router, b_router,
          sg_wt, chan, rows, consts, out):
    ctx = ExitStack()
    with ctx:
        def sb(name, shape, dt=F32):
            return ctx.enter_context(nc.sbuf_tensor(name, shape, dt))

        def sem(name):
            return ctx.enter_context(nc.semaphore(name))

        ring = sb("ring", [P, RING, SLOT])
        x_tok = sb("x_tok", [P, TT, D])
        u_ch = sb("u_ch", [P, KD, T])
        row_buf = sb("row_buf", [P, 3, D])
        gate_row = sb("gate_row", [P, 2, D])
        chan_sb = sb("chan_sb", [P, DEPTH, N_CHAN, KD])
        mod = sb("mod", [P, 4, KD])
        c_act = sb("c_act", [P, KD])
        ada_sum = sb("ada_sum", [P, 2, HALF])
        ones = sb("ones", [P, P])
        mean_w = sb("mean_w", [P, P])
        ident = sb("ident", [P, P])
        prec = sb("prec", [P, P])
        router_sb = sb("router_sb", [P, KD, EXPERTS])
        brout_sb = sb("brout_sb", [P, EXPERTS])
        eps = sb("eps", [P, 1])
        stats = sb("stats", [P, TT, 2, 6])
        aggr = sb("aggr", [P, TT, 2])
        std = sb("std", [P, TT])
        rstd = sb("rstd", [P, TT])
        blocks_i = sb("blocks_i", [1, EXPERTS], I32)
        start_i = sb("start_i", [1, EXPERTS], I32)
        CV_PAD = CV_TAPS - 1
        SC_PAD = SC_TAPS - 1
        cv_in_n, sc_in_n, full = KD * (T + CV_PAD), KD * (T + SC_PAD), KD * T
        shared_n = 5 * full + cv_in_n + sc_in_n + 2 * BANK + HEADS * P
        shared = sb("shared", [P, shared_n])
        at = [0]

        def part(n):
            at[0] += n
            return shared[:, at[0] - n:at[0]]

        gate_a = part(full).rearrange("p (k t) -> p k t", k=KD)
        sc_part = part(sc_in_n)
        sc_in = sc_part.rearrange("p (k t) -> p k t", k=KD)
        gate_b = sc_part[:, 0:full].rearrange("p (k t) -> p k t", k=KD)
        y_a = part(full).rearrange("p (k t) -> p k t", k=KD)
        cv_part = part(cv_in_n)
        cv_in = cv_part.rearrange("p (k t) -> p k t", k=KD)
        cv_sq = cv_part[:, 0:full].rearrange("p (k t) -> p k t", k=KD)
        y_b = part(full).rearrange("p (k t) -> p k t", k=KD)
        y_c = part(full).rearrange("p (k t) -> p k t", k=KD)
        sg_flat = part(full)
        sg_v = sg_flat.rearrange("p (n c) -> p n c", n=TT)
        merged = sg_flat.rearrange("p (k t) -> p k t", k=KD)
        tmp = part(2 * BANK).rearrange("p (b n) -> p b n", b=2)
        sg_wm = part(HEADS * P).rearrange("p (h t) -> p h t", h=HEADS)
        glu_sig = gate_a
        cv_mean, cv_std, cv_rstd = (cv_part[:, i * T:(i + 1) * T] for i in range(3))

        at[0] = 0
        SORTED = SLOTS + BLOCK
        sorted_ch = part(KD * SORTED).rearrange("p (k s) -> p k s", k=KD)
        onehot = part(TT * SLOTS).rearrange("p (n s) -> p n s", n=TT)
        iota = part(SLOTS)
        tri16 = part(EXPERTS * EXPERTS).rearrange("p (a b) -> p a b", a=EXPERTS)
        xe = part(KD * BLOCK).rearrange("p (k s) -> p k s", k=KD)
        silu_e = part(T)
        hid = part(T)
        turned = part(BANK)
        y_e = part(BANK)
        pick = part(TT * P).rearrange("p (n d s) -> p n d s", n=TT, d=2)
        r_small = part(24 * TT * EXPERTS).rearrange("p (v n e) -> p v n e", v=24, n=TT)
        r_wide = part(3 * EXPERTS * EXPERTS).rearrange("p (v n) -> p v n", v=3)
        assert at[0] <= shared_n

        psum = [ctx.enter_context(nc.psum_tensor(f"bank{b}", [P, BANK], F32)) for b in range(BANKS)]
        moe_sum = [[psum[2 * n + h] for h in range(2)] for n in range(TT)]
        ps_h1, ps_h3, ps_turn, ps_y = psum[4], psum[5], psum[6], psum[7]

        params_in = sem("params_in")
        consts_ready = sem("consts_ready")
        c_ready = sem("c_ready")
        unit_in = [sem(f"unit_in{s}") for s in range(RING)]
        bank_full = sem("bank_full")
        drained = {"act": sem("act_drained"), "dve": sem("dve_drained")}
        chain = sem("chain")
        ada_ready = sem("ada_ready")
        conv_step = sem("conv_step")
        rows_in, gates_in, sgw_in, moe_consts_in = sem("rows_in"), sem("gates_in"), sem("sgw_in"), sem("moe_consts_in")
        pads_ready = sem("pads_ready")
        sgw_masked = sem("sgw_masked")
        sgv_ready = sem("sgv_ready")
        ln_var, ln_std = sem("ln_var"), sem("ln_std")
        ln1_done = sem("ln1_done")
        yc_ready = sem("yc_ready")
        cv_ready, cv_centred, cv_squared, cv_normed, yb_ready = (
            sem("cv_ready"), sem("cv_centred"), sem("cv_squared"), sem("cv_normed"), sem("yb_ready"))
        merged_ready = sem("merged_ready")
        max_ready, exp_ready = sem("max_ready"), sem("exp_ready")
        mask_ready, onehot_ready, blocks_ready = sem("mask_ready"), sem("onehot_ready"), sem("blocks_ready")
        moe_zeroed, pos_step = sem("moe_zeroed"), sem("pos_step")
        xe_ready, pick_ready = sem("xe_ready"), sem("pick_ready")
        h1_ready, h3_ready, silu_ready, hid_ready = sem("h1_ready"), sem("h3_ready"), sem("silu_ready"), sem("hid_ready")
        turn_ready, turned_ready, y_ready, y_copied = sem("turn_ready"), sem("turned_ready"), sem("y_ready"), sem("y_copied")
        moe_ready, ln2_done, out_done = sem("moe_ready"), sem("ln2_done"), sem("out_done")

        passed = {e: sem(f"passed_{e}") for e in ("SP", "Pool", "DVE")}

        ada_v = w_ada.rearrange("l (k p) n -> l p k n", p=P)
        in_v = w_in.rearrange("l (k p) n -> l p k n", p=P)
        gate_v = w_gate.rearrange("l (k p) b n -> l p k b n", p=P)
        branch_v = w_branch.rearrange("l b (k p) n -> l b p k n", p=P)
        o_v = w_o.rearrange("l (k p) n -> l p k n", p=P)
        w1_v = w1.rearrange("l e (k p) f -> l e p k f", p=P)
        w3_v = w3.rearrange("l e (k p) f -> l e p k f", p=P)
        w2_v = w2.rearrange("l e (k p) n -> l e p k n", p=P)

        def slot(s, k=KD):
            return ring[:, s, :].rearrange("p (k n) -> p k n", k=k)

        def unit_dram(u, l):
            what, n = UNITS[u]
            cols = lambda i: slice(i * HALF, (i + 1) * HALF)
            if what == "ada":
                return ada_v[l][:, :, cols(n)]
            if what == "in":
                return in_v[l][:, :, cols(n)]
            if what == "gate":
                return gate_v[l][:, :, n[0], cols(n[1])]
            if what == "branch":
                return branch_v[l, n[0]][:, :, cols(n[1])]
            return o_v[l][:, :, cols(n)]

        def alone(eng):
            eng.sem_inc(passed[eng.engine.name], 1)

        def unit_loaded(eng, l, u):
            eng.wait_ge(unit_in[u % RING], 16 * (l * PER_SLOT[u % RING] + u // RING + 1))

        def unit_read(eng, l, u):
            what, n = UNITS[u]
            if what == "ada":
                eng.wait_ge(ada_ready, len(ADA_PARTS) * l + n + 1)
            else:
                filled(eng, l, (what, n, 1))

        def filled(eng, l, what):
            eng.wait_ge(bank_full, l * N_USES + USE[what] + 1)

        def after_drain(eng, l, what):
            who, n = DRAINED[what]
            eng.wait_ge(drained[who], l * N_DRAINED[who] + n)

        def bank(what):
            return psum[USE[what] % BANKS]

        block = ctx.enter_context(nc.Block())

        @block.sync
        def _(sp):
            sp.dma_start(c_act[:], c_cols).then_inc(params_in, 16)
            sp.dma_start(x_tok[:], x.rearrange("(n p) d -> p n d", p=P)).then_inc(params_in, 16)
            sp.dma_start(ident[:], consts[:, C_ID:C_ID + P]).then_inc(params_in, 16)
            sp.dma_start(chan_sb[:], chan).then_inc(params_in, 16)
            sp.dma_start(prec[:], consts[:, C_PREC:C_PREC + P]).then_inc(params_in, 16)
            sp.dma_start(router_sb[:], w_router.rearrange("(k p) e -> p k e", p=P)).then_inc(params_in, 16)
            sp.dma_start(brout_sb[:], b_router.partition_broadcast(P)).then_inc(params_in, 16)
            done = sp.alloc_register("blocks_done")
            sp.reg_mov(done, PRIMED)
            with sp.Fori(0, DEPTH) as l:
                for u in range(len(UNITS)):
                    if u < RING:
                        sp.wait_ge(y_ready, sp.snap(done))
                    else:
                        unit_read(sp, l, u - RING)
                    alone(sp)
                    sp.dma_start(slot(u % RING), unit_dram(u, l)).then_inc(unit_in[u % RING], 16)

                def expert(e, s0, wait):
                    for i, (src, k) in enumerate(((w1_v, KD), (w3_v, KD), (w2_v, KE))):
                        wait(s0 + i)
                        alone(sp)
                        sp.dma_start(slot(s0 + i, k), src[l, e]).then_inc(unit_in[s0 + i], 16)

                for e in range(2):
                    expert(e, 3 * e, lambda s: unit_read(sp, l, max(range(s, len(UNITS), RING))))
                sp.wait_ge(blocks_ready, l + 1)
                alone(sp)
                with sp.Fori(1, MOE_PAIRS) as pair:
                    for q in range(2):
                        n = sp.value_load(blocks_i[0:1, bass.ds(2 * pair + (q - 2), 1)], min_val=1, max_val=T // BLOCK)
                        sp.reg_add(done, done, n)
                        expert(2 * pair + q, 3 * q, lambda s: sp.wait_ge(y_ready, sp.snap(done)))
                for e in (EXPERTS - 2, EXPERTS - 1):
                    n = sp.value_load(blocks_i[0:1, e:e + 1], min_val=1, max_val=T // BLOCK)
                    sp.reg_add(done, done, n)
            sp.wait_ge(ln2_done, DEPTH * TT + PRIMED)
            sp.dma_start(out.rearrange("(n p) d -> p n d", p=P), x_tok[:]).then_inc(out_done, 16)
            sp.wait_ge(out_done, 16)

        @block.gpsimd
        def _(pool):
            nc.gpsimd.memset(ones[:], 1.0).then_inc(consts_ready, 1)
            nc.gpsimd.memset(mean_w[:], 1.0 / D).then_inc(consts_ready, 1)
            nc.gpsimd.memset(eps[:], LN_EPS).then_inc(consts_ready, 1)
            with pool.Fori(0, DEPTH) as l:
                pool.wait_ge(ln2_done, l * TT + PRIMED)
                pool.dma_start(row_buf[:, 0:3, :], rows[l, ROW_SG:ROW_SG + 3].partition_broadcast(P)).then_inc(rows_in, 16)
                pool.dma_start(gate_row[:, :, :], rows[l, ROW_GATE:ROW_GATE + 2].partition_broadcast(P)).then_inc(gates_in, 16)
                pool.dma_start(sg_wm, sg_wt[l]).then_inc(sgw_in, 16)
                nc.gpsimd.memset(cv_in[:, :, 0:CV_PAD], 0.0).then_inc(pads_ready, 1)
                nc.gpsimd.memset(sc_in[:, :, 0:SC_PAD], 0.0).then_inc(pads_ready, 1)
                pool.wait_ge(sgw_in, 16 * (l + 1))
                alone(pool)
                nc.gpsimd.affine_select(out=sg_wm, in_=sg_wm, compare_op=ALU.is_ge, fill=0.0, base=0,
                                        pattern=[[0, HEADS], [1, P]], channel_multiplier=-1).then_inc(sgw_masked, 1)
                pool.wait_ge(yc_ready, (HEADS // 2) * (l + 1))
                pool.dma_start(row_buf[:, 0:2, :], rows[l, ROW_LN1:ROW_LN1 + 2].partition_broadcast(P)).then_inc(rows_in, 16)
                pool.wait_ge(ln1_done, TT * (l + 1))
                pool.dma_start(row_buf[:, 0:2, :], rows[l, ROW_LN2:ROW_LN2 + 2].partition_broadcast(P)).then_inc(rows_in, 16)
                pool.dma_start(iota, consts[:, C_IOTA:C_IOTA + SLOTS]).then_inc(moe_consts_in, 16)
                pool.dma_start(tri16, consts[:, C_TRI16:C_IOTA].rearrange("p (a b) -> p a b", a=EXPERTS)).then_inc(moe_consts_in, 16)
                nc.gpsimd.memset(sorted_ch[:, :, SLOTS:SORTED], 0.0).then_inc(moe_zeroed, 1)
                nc.gpsimd.memset(y_e, 0.0).then_inc(moe_zeroed, 1)
                nc.gpsimd.memset(turned, 0.0).then_inc(moe_zeroed, 1)

        @block.scalar
        def _(act):
            act.wait_ge(params_in, 16 * 7)
            nc.scalar.activation(c_act[:], c_act[:], ACT.Silu).then_inc(c_ready, 1)
            act.wait_ge(consts_ready, 3)
            n_blk = act.alloc_register("act_block")
            act.reg_mov(n_blk, PRIMED)
            act.sem_inc(silu_ready, PRIMED)
            act.sem_inc(turned_ready, PRIMED)
            act.sem_inc(y_copied, PRIMED)

            def turn(l, name, which, shift, scale):
                for i in range(0, KD // 2, 2):
                    filled(act, l, (name, i))
                    for j in range(2):
                        k = 2 * i + j
                        ins = nc.scalar.activation(u_ch[:, k, :], bank((name, i))[:, j * T:(j + 1) * T], ACT.Identity,
                                                   bias=mod[:, shift, k:k + 1], scale=mod[:, scale, k:k + 1])
                    ins.then_inc(drained["act"], 1)

            def pairs(l, unit, dst, func):
                for i in range(2):
                    filled(act, l, (*unit, i))
                    nc.scalar.activation(dst(i), bank((*unit, i))[:], func).then_inc(drained["act"], 1)

            def two(buf, col, i):
                k = MT * col + 2 * i
                return buf[:, k:k + 2, :].rearrange("p k t -> p (k t)")

            def gates(l, b, dst):
                for col in range(2):
                    for i in range(2):
                        filled(act, l, ("gate", (b, col), i))
                        for j in range(2):
                            k = MT * col + 2 * i + j
                            ins = nc.scalar.activation(dst[:, k, :], bank(("gate", (b, col), i))[:, j * T:(j + 1) * T],
                                                       ACT.Sigmoid, bias=chan_at(l, B_GATE + b, k))
                        ins.then_inc(drained["act"], 1)

            def chan_at(l, v, k):
                return chan_sb[:, bass.ds(l, 1), v, k:k + 1].rearrange("p a b -> p (a b)")

            def deviation(l, n):
                act.wait_ge(ln_var, 3 * l + n + 1)
                nc.scalar.activation(std[:], aggr[:, :, 1], ACT.Sqrt, bias=eps[:, 0:1]).then_inc(ln_std, 1)

            with act.Fori(0, DEPTH) as l:
                after_drain(act, l, ("ada", 3))
                turn(l, "turn1", 0, SHIFT1, SCALE1)
                pairs(l, ("in", 8), lambda i: two(glu_sig, 0, i), ACT.Sigmoid)
                pairs(l, ("in", 9), lambda i: two(glu_sig, 1, i), ACT.Sigmoid)
                for h in range(2):
                    pairs(l, ("in", 12 + h), lambda i: sg_v[:, i, h * HALF:(h + 1) * HALF], ACT.Gelu_apprx_tanh)
                deviation(l, 0)
                for col in range(2):
                    pairs(l, ("in", 2 + col), lambda i: two(y_a, col, i), ACT.Copy)
                for col in range(2):
                    pairs(l, ("in", 10 + col), lambda i: two(y_c, col, i), ACT.Gelu_apprx_tanh)
                gates(l, 0, gate_a)
                after_drain(act, l, ("in", 1, 1))
                gates(l, 2, gate_b)
                act.wait_ge(cv_centred, l + 1)
                nc.scalar.activation(cv_sq, y_b, ACT.Square).then_inc(cv_squared, 1)
                filled(act, l, ("var", 0))
                nc.scalar.activation(cv_std, bank(("var", 0))[:, 0:T], ACT.Sqrt, bias=eps[:, 0:1]).then_inc(drained["act"], 1)
                after_drain(act, l, ("branch", (0, 1), 1))
                gates(l, 1, gate_a)
                act.wait_ge(cv_normed, l + 1)
                for k in range(KD):
                    ins = nc.scalar.activation(y_b[:, k, :], y_b[:, k, :], ACT.Silu, bias=chan_at(l, CV_LB, k),
                                               scale=chan_at(l, CV_G, k))
                ins.then_inc(yb_ready, 1)
                deviation(l, 1)
                turn(l, "turn2", 0, SHIFT2, SCALE2)
                act.wait_ge(max_ready, l + 1)
                nc.scalar.activation(r_small[:, 1], r_small[:, 0], ACT.Exp).then_inc(exp_ready, 1)
                for k in range(0, KD, 2):
                    filled(act, l, ("gather", k))
                    nc.scalar.activation(sorted_ch[:, k, 0:SLOTS], bank(("gather", k))[:], ACT.Identity,
                                         bias=mod[:, SHIFT2, k:k + 1],
                                         scale=mod[:, SCALE2, k:k + 1]).then_inc(drained["act"], 1)
                act.wait_ge(blocks_ready, l + 1)
                act.wait_ge(moe_zeroed, 3 * (l + 1))
                with act.Fori(0, EXPERTS) as e:
                    n = act.value_load(blocks_i[0:1, bass.ds(e, 1)], min_val=1, max_val=T // BLOCK)
                    with act.Fori(0, n):
                        b = act.snap(n_blk)
                        act.wait_ge(h1_ready, b + 1)
                        nc.scalar.activation(silu_e, ps_h1[:, 0:T], ACT.Silu).then_inc(silu_ready, 1)
                        act.wait_ge(turn_ready, b + 1)
                        nc.scalar.activation(turned, ps_turn[:], ACT.Copy).then_inc(turned_ready, 1)
                        act.wait_ge(y_ready, b + 1)
                        nc.scalar.activation(y_e, ps_y[:], ACT.Copy).then_inc(y_copied, 1)
                        act.reg_add(n_blk, n_blk, 1)
                deviation(l, 2)

        @block.vector
        def _(dve):
            v = nc.vector
            steps = [0]
            n_blk = dve.alloc_register("dve_block")
            dve.reg_mov(n_blk, PRIMED)
            dve.sem_inc(xe_ready, PRIMED)
            dve.sem_inc(pick_ready, PRIMED)
            dve.sem_inc(hid_ready, PRIMED)
            dve.sem_inc(ln2_done, PRIMED)

            def chan_at(l, n, k):
                return chan_sb[:, bass.ds(l, 1), n, k:k + 1].rearrange("p a b -> p (a b)")

            def then(l, ins):
                steps[0] += 1
                ins.then_inc(chain, 1)
                dve.wait_ge(chain, l * DVE_CHAIN + steps[0])

            def drain(ins):
                ins.then_inc(drained["dve"], 1)

            def ada_unit(l, n):
                u = UNIT[("ada", n)]
                unit_loaded(dve, l, u)
                if n >= 2:
                    filled(dve, l, ("ada", n - 2))
                acc, w = ada_sum[:, n % 2, :], slot(u % RING)
                then(l, v.tensor_scalar(acc, w[:, 0, :], c_act[:, 0:1], None, ALU.mult))
                for k in range(1, KD - 1):
                    then(l, v.scalar_tensor_tensor(out=acc, in0=w[:, k, :], scalar=c_act[:, k:k + 1], in1=acc,
                                                   op0=ALU.mult, op1=ALU.add))
                k = KD - 1
                ins = v.scalar_tensor_tensor(out=acc, in0=w[:, k, :], scalar=c_act[:, k:k + 1], in1=acc,
                                             op0=ALU.mult, op1=ALU.add)
                ins.then_inc(ada_ready, 1)

            def ada_out(l, n):
                part, half = ADA_PARTS[n], n % 2
                ps = bank(("ada", n))
                filled(dve, l, ("ada", n))
                if part in (2, 5):
                    row = gate_row[:, part // 5, half * HALF:(half + 1) * HALF]
                    dve.wait_ge(gates_in, 16 * (l + 1))
                    drain(v.tensor_tensor(row, ps[:], row, ALU.add))
                else:
                    m = {0: SHIFT1, 1: SCALE1, 3: SHIFT2, 4: SCALE2}[part]
                    b = chan_sb[:, bass.ds(l, 1), m, half * MT:(half + 1) * MT].rearrange("p a b -> p (a b)")
                    drain(v.scalar_tensor_tensor(out=mod[:, m, half * MT:(half + 1) * MT], in0=ps[:, 0:MT],
                                                 scalar=1.0 if part in (1, 4) else 0.0, in1=b,
                                                 op0=ALU.add, op1=ALU.add))

            def turn(l, name, shift, scale):
                for i in range(1, KD // 2, 2):
                    filled(dve, l, (name, i))
                    for j in range(2):
                        k = 2 * i + j
                        ins = v.tensor_scalar(u_ch[:, k, :], bank((name, i))[:, j * T:(j + 1) * T],
                                              mod[:, scale, k:k + 1], mod[:, shift, k:k + 1], ALU.mult, ALU.add)
                    drain(ins)

            def conv31(l, pair, nth):
                tiles = (2 * pair, 2 * pair + 1)
                base = l * (KD * CV_TAPS) + 2 * nth * CV_TAPS

                def step(j, a, at):
                    k = tiles[a]
                    if isinstance(j, int) and j == 0:
                        return v.tensor_scalar(y_b[:, k, :], cv_in[:, k, 0:T], chan_at(l, CV_W, k),
                                               chan_at(l, CV_B, k), ALU.mult, ALU.add).then_inc(conv_step, 1)
                    w = chan_sb[:, bass.ds(l, 1), bass.ds(j + CV_W, 1), k:k + 1].rearrange("p a b c -> p (a b c)")
                    dve.wait_ge(conv_step, at)
                    return v.scalar_tensor_tensor(out=y_b[:, k, :], in0=cv_in[:, k, bass.ds(j, T)], scalar=w,
                                                  in1=y_b[:, k, :], op0=ALU.mult, op1=ALU.add).then_inc(conv_step, 1)

                for a in range(2):
                    step(0, a, 0)
                unroll = 5
                with dve.Fori(0, (CV_TAPS - 1) // unroll) as r:
                    for i in range(unroll):
                        for a in range(2):
                            step(r * unroll + (i + 1), a, base + 2 * unroll * r + (2 * i + a + 1))

            def conv3(l, pair):
                for a in range(2):
                    k = 2 * pair + a
                    v.tensor_scalar(y_a[:, k, :], sc_in[:, k, 0:T], chan_at(l, SC_W, k), None,
                                    ALU.mult).then_inc(chain, 1)
                steps[0] += 2
                dve.wait_ge(chain, l * DVE_CHAIN + steps[0])
                for j in range(1, SC_TAPS):
                    for a in range(2):
                        k = 2 * pair + a
                        v.scalar_tensor_tensor(out=y_a[:, k, :], in0=sc_in[:, k, j:j + T],
                                               scalar=chan_at(l, SC_W + j, k), in1=y_a[:, k, :],
                                               op0=ALU.mult, op1=ALU.add).then_inc(chain, 1)
                    steps[0] += 2
                    dve.wait_ge(chain, l * DVE_CHAIN + steps[0])

            def flat(buf, col, i):
                k = MT * col + 2 * i
                return buf[:, k:k + 2, :]

            def ps2(what):
                return bank(what)[:].rearrange("p (k t) -> p k t", k=2)

            def norm_rows(l, n, buf, row_in, signal, gain=0):
                alone(dve)
                for t in range(TT):
                    ins = v.bn_aggr(aggr[:, t, :], stats[:, t].rearrange("p h s -> p (h s)"))
                ins.then_inc(ln_var, 1)
                dve.wait_ge(ln_std, 3 * l + n + 1)
                then(l, v.reciprocal(rstd[:], std[:]))
                dve.wait_ge(rows_in, row_in)
                for t in range(TT):
                    then(l, v.tensor_scalar(buf[:, t, :], buf[:, t, :], aggr[:, t, 0:1], rstd[:, t:t + 1],
                                            ALU.subtract, ALU.mult))
                    then(l, v.tensor_tensor(buf[:, t, :], buf[:, t, :], row_buf[:, 0, :], ALU.mult))
                    v.tensor_tensor(buf[:, t, :], buf[:, t, :], row_buf[:, 1, :], ALU.add).then_inc(signal, 1)

            def residual(l, ps, gate, t, h):
                xs = x_tok[:, t, h * HALF:(h + 1) * HALF]
                v.tensor_tensor(tmp[:, 0, :], ps[:], gate_row[:, gate, h * HALF:(h + 1) * HALF], ALU.mult).then_inc(chain, 1)
                steps[0] += 1
                dve.wait_ge(chain, l * DVE_CHAIN + steps[0])
                then(l, v.scalar_tensor_tensor(out=xs, in0=xs, scalar=ALPHA, in1=tmp[:, 0, :],
                                               op0=ALU.mult, op1=ALU.add))
                return v.bn_stats(stats[:, t, h, :], xs)

            dve.wait_ge(params_in, 16 * 7)
            dve.wait_ge(c_ready, 1)
            with dve.Fori(0, DEPTH) as l:
                steps[0] = 0
                for n in range(4):
                    ada_unit(l, n)
                    if n:
                        ada_out(l, n - 1)
                ada_out(l, 3)
                turn_wait = DRAINED[("ada", 3)][1]
                dve.wait_ge(drained["dve"], l * N_DRAINED["dve"] + turn_wait)
                turn(l, "turn1", SHIFT1, SCALE1)

                dve.wait_ge(pads_ready, 2 * (l + 1))
                for col in range(2):
                    after_drain(dve, l, ("in", 8 + col, 1))
                    for i in range(2):
                        what = ("in", 6 + col, i)
                        filled(dve, l, what)
                        k = MT * col + 2 * i
                        drain(v.tensor_tensor(cv_in[:, k:k + 2, CV_PAD:CV_PAD + T], ps2(what), flat(glu_sig, col, i), ALU.mult))
                    dve.wait_ge(drained["dve"], l * N_DRAINED["dve"] + DRAINED[("in", 6 + col, 1)][1])
                    conv31(l, 2 * col, col)

                for h in range(2):
                    ada_unit(l, 4 + h)
                after_drain(dve, l, ("in", 13, 1))
                for t in range(TT):
                    for h in range(2):
                        ins = v.bn_stats(stats[:, t, h, :], sg_v[:, t, h * HALF:(h + 1) * HALF])
                then(l, ins)
                norm_rows(l, 0, sg_v, 48 * l + 16, sgv_ready)
                ada_out(l, 4)
                ada_out(l, 5)

                for col in range(2):
                    after_drain(dve, l, ("in", 2 + col, 1))
                    for i in range(2):
                        what = ("in", 4 + col, i)
                        filled(dve, l, what)
                        k = MT * col + 2 * i
                        drain(v.tensor_tensor(sc_in[:, k:k + 2, SC_PAD:SC_PAD + T], ps2(what), flat(y_a, col, i), ALU.mult))
                    dve.wait_ge(drained["dve"], l * N_DRAINED["dve"] + DRAINED[("in", 4 + col, 1)][1])
                    if col == 0:
                        ada_unit(l, 6)
                    conv31(l, 2 * col + 1, 2 + col)
                    if col == 0:
                        ada_out(l, 6)
                    for i in range(2):
                        conv3(l, 2 * col + i)
                ada_unit(l, 7)
                ada_out(l, 7)
                for col in range(2):
                    for i in range(2):
                        what = ("in", col, i)
                        filled(dve, l, what)
                        ins = v.tensor_tensor(flat(y_a, col, i), ps2(what), flat(y_a, col, i), ALU.mult)
                        drain(ins)
                ada_unit(l, 8)
                ada_out(l, 8)
                ada_unit(l, 9)
                ada_out(l, 9)
                after_drain(dve, l, ("in", 11, 1))
                for i in range(HEADS // 2):
                    what = ("mix", i)
                    filled(dve, l, what)
                    if i >= 2:
                        dve.wait_ge(yc_ready, (HEADS // 2) * l + i - 1)
                    srow = row_buf[:, 2, :].rearrange("p (h t) -> p h t", h=HEADS)
                    o4 = tmp[:, i % 2, :].rearrange("p (h n t) -> p h n t", h=2, n=TT)
                    drain(v.tensor_tensor(o4, bank(what)[:].rearrange("p (h n t) -> p h n t", h=2, n=TT),
                                          srow[:, 2 * i:2 * i + 2, :].unsqueeze(2).broadcast_to([P, 2, TT, P]), ALU.add))
                    dve.wait_ge(drained["dve"], l * N_DRAINED["dve"] + DRAINED[what][1])
                    yc = y_c[:, 2 * i:2 * i + 2, :].rearrange("p k t -> p (k t)")
                    v.tensor_tensor(yc, yc, tmp[:, i % 2, :], ALU.mult).then_inc(yc_ready, 1)

                def branch(b, gate, first):
                    for col in range(2):
                        after_drain(dve, l, ("gate", (b, col), 1))
                        for i in range(2):
                            what = ("branch", (b, col), i)
                            filled(dve, l, what)
                            if first:
                                drain(v.tensor_tensor(flat(merged, col, i), ps2(what), flat(gate, col, i), ALU.mult))
                            else:
                                t2 = tmp[:, i, :].rearrange("p (k t) -> p k t", k=2)
                                drain(v.tensor_tensor(t2, ps2(what), flat(gate, col, i), ALU.mult))
                                dve.wait_ge(drained["dve"], l * N_DRAINED["dve"] + DRAINED[what][1])
                                ins = v.tensor_tensor(flat(merged, col, i), flat(merged, col, i), t2, ALU.add)
                                if b == 1:
                                    ins.then_inc(merged_ready, 1)
                                else:
                                    then(l, ins)

                ada_unit(l, 10)
                ada_out(l, 10)
                branch(0, gate_a, True)
                ada_unit(l, 11)
                ada_out(l, 11)
                branch(2, gate_b, False)
                filled(dve, l, ("mean", 0))
                drain(v.tensor_copy(cv_mean, bank(("mean", 0))[:, 0:T]))
                dve.wait_ge(drained["dve"], l * N_DRAINED["dve"] + DRAINED[("mean", 0)][1])
                v.tensor_tensor(y_b, y_b, cv_mean.unsqueeze(1).broadcast_to([P, KD, T]), ALU.subtract).then_inc(cv_centred, 1)
                after_drain(dve, l, ("var", 0))
                then(l, v.reciprocal(cv_rstd, cv_std))
                v.tensor_tensor(y_b, y_b, cv_rstd.unsqueeze(1).broadcast_to([P, KD, T]), ALU.mult).then_inc(cv_normed, 1)
                branch(1, gate_a, False)

                for h in range(2):
                    for t in range(TT):
                        filled(dve, l, ("o", h, t))
                        drain(residual(l, bank(("o", h, t)), 0, t, h))
                dve.wait_ge(drained["dve"], l * N_DRAINED["dve"] + DRAINED[("o", 1, 1)][1])
                norm_rows(l, 1, x_tok, 48 * l + 32, ln1_done)
                turn(l, "turn2", SHIFT2, SCALE2)

                def small(i):
                    return r_small[:, i]

                def groups(a):
                    return a.rearrange("p n (g e) -> p (n g) e", g=GROUPS)

                def over(ap, dim, shape):
                    return ap.unsqueeze(dim).broadcast_to(shape)

                LOG, EXP, SCORE, SEL, CHOSEN, CS, MASK, MS, G, PREF, DST, POS, W0 = range(13)
                filled(dve, l, ("logits", 0))
                drain(v.tensor_copy(small(LOG), bank(("logits", 0))[:, 0:TT * EXPERTS].rearrange("p (n e) -> p n e", n=TT)))
                dve.wait_ge(drained["dve"], l * N_DRAINED["dve"] + DRAINED[("logits", 0)][1])
                red = r_small[:, W0]
                then(l, v.tensor_reduce(red[:, 0, 0:TT], small(LOG), AX_X, ALU.max))
                v.tensor_tensor(small(LOG), small(LOG), over(red[:, 0, 0:TT], 2, [P, TT, EXPERTS]), ALU.subtract).then_inc(max_ready, 1)
                dve.wait_ge(exp_ready, l + 1)
                then(l, v.tensor_reduce(red[:, 0, 2:2 + TT], small(EXP), AX_X, ALU.add))
                then(l, v.reciprocal(red[:, 0, 4:4 + TT], red[:, 0, 2:2 + TT]))
                then(l, v.tensor_tensor(small(SCORE), small(EXP), over(red[:, 0, 4:4 + TT], 2, [P, TT, EXPERTS]), ALU.mult))
                then(l, v.tensor_tensor(small(SEL), small(SCORE), brout_sb[:].unsqueeze(1).broadcast_to([P, TT, EXPERTS]), ALU.add))
                dve.wait_ge(moe_consts_in, 32 * (l + 1))

                def beaten(src, rows_n, out_ap, gt, eq):
                    four = [P, rows_n, PER_GROUP, PER_GROUP]
                    other, own = src.unsqueeze(2).broadcast_to(four), src.unsqueeze(3).broadcast_to(four)
                    tri = tri16[:, 0:PER_GROUP, 0:PER_GROUP]
                    n = rows_n * PER_GROUP * PER_GROUP
                    g4 = r_wide[:, gt, 0:n].rearrange("p (r a b) -> p r a b", r=rows_n, a=PER_GROUP)
                    e4 = r_wide[:, eq, 0:n].rearrange("p (r a b) -> p r a b", r=rows_n, a=PER_GROUP)
                    then(l, v.tensor_tensor(g4, other, own, ALU.is_gt))
                    then(l, v.tensor_tensor(e4, other, own, ALU.is_equal))
                    then(l, v.tensor_tensor(e4, e4, tri.unsqueeze(1).broadcast_to(four), ALU.mult))
                    then(l, v.tensor_tensor(g4, g4, e4, ALU.add))
                    then(l, v.tensor_reduce(out_ap, g4, AX_X, ALU.add))

                rank = r_small[:, W0 + 1]
                beaten(groups(small(SEL)), TT * GROUPS, groups(rank), 0, 1)
                then(l, v.tensor_scalar(small(CHOSEN), rank, TOP_K - 0.5, None, ALU.is_lt))
                then(l, v.tensor_tensor(small(CS), small(CHOSEN), small(SEL), ALU.mult))
                gscore = red[:, 1, 0:TT * GROUPS]
                then(l, v.tensor_reduce(gscore, groups(small(CS)), AX_X, ALU.add))
                grank = red[:, 1, TT * GROUPS:2 * TT * GROUPS]
                beaten(gscore.rearrange("p (n g) -> p n g", n=TT), TT, grank.rearrange("p (n g) -> p n g", n=TT), 0, 1)
                then(l, v.tensor_scalar(grank, grank, 0.5, None, ALU.is_lt))
                then(l, v.tensor_tensor(groups(small(MASK)), groups(small(CHOSEN)),
                                        grank.unsqueeze(2).broadcast_to([P, TT * GROUPS, PER_GROUP]), ALU.mult))
                v.tensor_tensor(small(MS), small(MASK), small(SCORE), ALU.mult).then_inc(mask_ready, 1)
                dve.wait_ge(mask_ready, l + 1)
                then(l, v.tensor_reduce(red[:, 0, 6:6 + TT], small(MS), AX_X, ALU.add))
                then(l, v.reciprocal(red[:, 0, 8:8 + TT], red[:, 0, 6:6 + TT]))
                then(l, v.tensor_tensor(small(G), small(MS), over(red[:, 0, 8:8 + TT], 2, [P, TT, EXPERTS]), ALU.mult))
                filled(dve, l, ("ranks", 0))
                rk = bank(("ranks", 0))
                count = r_small[:, W0 + 2, 0]
                v.tensor_copy(small(PREF), rk[:, 0:TT * EXPERTS].rearrange("p (n e) -> p n e", n=TT))
                drain(v.tensor_copy(count, rk[:, TT * EXPERTS:(TT + 1) * EXPERTS]))
                dve.wait_ge(drained["dve"], l * N_DRAINED["dve"] + DRAINED[("ranks", 0)][1])
                start = r_small[:, W0 + 2, 1]
                s16 = r_wide[:, 2].rearrange("p (a b) -> p a b", a=EXPERTS)
                then(l, v.tensor_tensor(s16, tri16, count.unsqueeze(1).broadcast_to([P, EXPERTS, EXPERTS]), ALU.mult))
                then(l, v.tensor_reduce(start, s16, AX_X, ALU.add))
                then(l, v.tensor_tensor(small(DST), small(PREF), start.unsqueeze(1).broadcast_to([P, TT, EXPERTS]), ALU.add))
                lo, hi = small(W0 + 3), small(W0 + 4)
                then(l, v.tensor_scalar(lo, small(DST), -BIG, None, ALU.add))
                then(l, v.tensor_tensor(lo, lo, small(MASK), ALU.mult))
                then(l, v.tensor_reduce(red[:, 0, 10:10 + TT], lo, AX_X, ALU.min))
                then(l, v.tensor_scalar(red[:, 0, 10:10 + TT], red[:, 0, 10:10 + TT], BIG, None, ALU.add))
                then(l, v.tensor_scalar(hi, small(DST), 1.0, None, ALU.add))
                then(l, v.tensor_tensor(hi, hi, small(MASK), ALU.mult))
                then(l, v.tensor_reduce(red[:, 0, 12:12 + TT], hi, AX_X, ALU.max))
                then(l, v.tensor_scalar(red[:, 0, 12:12 + TT], red[:, 0, 12:12 + TT], -1.0, None, ALU.add))
                for t in range(TT):
                    then(l, v.tensor_scalar(onehot[:, t, :], iota, red[:, 0, 10 + t:11 + t], None, ALU.is_equal))
                    v.scalar_tensor_tensor(out=onehot[:, t, :], in0=iota, scalar=red[:, 0, 12 + t:13 + t], in1=onehot[:, t, :],
                                           op0=ALU.is_equal, op1=ALU.add).then_inc(onehot_ready, 1)
                nb = r_small[:, W0 + 5, 0]
                then(l, v.tensor_scalar(nb, count, float(BLOCK), 1.0, ALU.is_gt, ALU.add))
                for i in range(2, T // BLOCK):
                    then(l, v.scalar_tensor_tensor(out=nb, in0=count, scalar=float(i * BLOCK), in1=nb,
                                                   op0=ALU.is_gt, op1=ALU.add))
                v.tensor_copy(start_i[:], start[0:1, :])
                v.tensor_copy(blocks_i[:], nb[0:1, :]).then_inc(blocks_ready, 1)
                then(l, v.scalar_tensor_tensor(out=small(POS), in0=small(PREF), scalar=1.0, in1=small(MASK),
                                               op0=ALU.add, op1=ALU.mult))
                v.tensor_scalar(small(POS), small(POS), -1.0, None, ALU.add).then_inc(pos_step, 1)
                for k in range(1, KD, 2):
                    filled(dve, l, ("gather", k))
                    drain(v.tensor_scalar(sorted_ch[:, k, 0:SLOTS], bank(("gather", k))[:], mod[:, SCALE2, k:k + 1],
                                          mod[:, SHIFT2, k:k + 1], ALU.mult, ALU.add))
                dve.wait_ge(drained["dve"], (l + 1) * N_DRAINED["dve"])
                after_drain(dve, l, ("gather", KD - 2))
                dve.wait_ge(moe_zeroed, 3 * (l + 1))
                dve.wait_ge(blocks_ready, l + 1)
                alone(dve)

                with dve.Fori(0, EXPERTS) as e:
                    n = dve.value_load(blocks_i[0:1, bass.ds(e, 1)], min_val=1, max_val=T // BLOCK)
                    first = dve.value_load(start_i[0:1, bass.ds(e, 1)], min_val=0, max_val=SLOTS)
                    with dve.Fori(0, n) as i:
                        b = dve.snap(n_blk)
                        dve.wait_ge(h3_ready, b)
                        at_s = nc.s_assert_within(first + i * BLOCK, 0, SLOTS)
                        v.tensor_copy(xe, sorted_ch[:, :, bass.ds(at_s, BLOCK)]).then_inc(xe_ready, 1)
                        dve.wait_ge(turn_ready, b)
                        dve.wait_ge(pos_step, b + l)
                        for t in range(TT):
                            pos_c = small(POS)[:, t, bass.ds(e, 1)]
                            g_c = small(G)[:, t, bass.ds(e, 1)]
                            ins = v.tensor_scalar(pick[:, t], iota[:, 0:BLOCK].unsqueeze(1).broadcast_to([P, 2, BLOCK]),
                                                  pos_c, g_c, ALU.is_equal, ALU.mult)
                        ins.then_inc(pick_ready, 1)
                        dve.wait_ge(pick_ready, b + 1)
                        col = small(POS)[:, :, bass.ds(e, 1)]
                        v.tensor_scalar(col, col, -float(BLOCK), None, ALU.add).then_inc(pos_step, 1)
                        dve.wait_ge(silu_ready, b + 1)
                        dve.wait_ge(h3_ready, b + 1)
                        v.tensor_tensor(hid, ps_h3[:, 0:T], silu_e, ALU.mult).then_inc(hid_ready, 1)
                        dve.reg_add(n_blk, n_blk, 1)

                dve.wait_ge(moe_ready, l + 1)
                for h in range(2):
                    for t in range(TT):
                        ins = residual(l, moe_sum[t][h], 1, t, h)
                then(l, ins)
                norm_rows(l, 2, x_tok, 48 * l + 48, ln2_done)
                assert steps[0] == DVE_CHAIN, steps[0]

        @block.tensor
        def _(pe):
            mm = nc.tensor.matmul
            n_blk = pe.alloc_register("pe_block")
            pe.reg_mov(n_blk, PRIMED)
            pe.sem_inc(h1_ready, PRIMED)
            pe.sem_inc(h3_ready, PRIMED)
            pe.sem_inc(turn_ready, PRIMED)
            pe.sem_inc(y_ready, PRIMED)

            def open_bank(l, what):
                i = USE[what]
                if i >= BANKS:
                    after_drain(pe, l, USES[i - BANKS][0])
                return psum[i % BANKS]

            def fill(what, ins):
                ins.then_inc(bank_full, 1)

            def ada(l, n):
                ps = open_bank(l, ("ada", n))
                pe.wait_ge(ada_ready, len(ADA_PARTS) * l + n + 1)
                acc = ada_sum[:, n % 2, :]
                if ADA_PARTS[n] in (2, 5):
                    ins = mm(ps[:], ones[:], acc, start=True, stop=True)
                else:
                    for m in range(MT):
                        ins = mm(ps[:, m:m + 1], acc[:, m * P:(m + 1) * P], ones[:, 0:1], start=True, stop=True)
                fill(("ada", n), ins)

            def channel_major(l, unit, src):
                u = UNIT[unit]
                unit_loaded(pe, l, u)
                w = slot(u % RING)
                for i in range(2):
                    ps = open_bank(l, (*unit, i))
                    for j in range(2):
                        m = 2 * i + j
                        for k in range(KD):
                            ins = mm(ps[:, j * T:(j + 1) * T], w[:, k, m * P:(m + 1) * P], src[:, k, :],
                                     start=(k == 0), stop=(k == KD - 1))
                    fill((*unit, i), ins)

            def token_major(l, unit, src):
                u = UNIT[unit]
                unit_loaded(pe, l, u)
                w = slot(u % RING)
                for t in range(TT):
                    ps = open_bank(l, (*unit, t))
                    for k in range(KD):
                        ins = mm(ps[:], src[:, k, t * P:(t + 1) * P], w[:, k, :], start=(k == 0), stop=(k == KD - 1))
                    fill((*unit, t), ins)

            def turn(l, name):
                for i in range(KD // 2):
                    ps = open_bank(l, (name, i))
                    for j in range(2):
                        for t in range(TT):
                            ins = nc.tensor.transpose(ps[:, j * T + t * P:j * T + (t + 1) * P],
                                                      x_tok[:, t, (2 * i + j) * P:(2 * i + j + 1) * P], ident[:])
                    fill((name, i), ins)
                after_drain(pe, l, (name, KD // 2 - 2))
                after_drain(pe, l, (name, KD // 2 - 1))

            pe.wait_ge(consts_ready, 3)
            pe.wait_ge(params_in, 16 * 7)
            with pe.Fori(0, DEPTH) as l:
                pe.wait_ge(ln2_done, l * TT + PRIMED)
                for n in range(4):
                    ada(l, n)
                turn(l, "turn1")
                for what, n in UNITS[4:]:
                    if (what, n) == ("gate", (0, 0)):
                        pe.wait_ge(sgv_ready, TT * (l + 1))
                        pe.wait_ge(sgw_masked, l + 1)
                        for i in range(HEADS // 2):
                            ps = open_bank(l, ("mix", i))
                            for j in range(2):
                                h = 2 * i + j
                                for t in range(TT):
                                    ins = mm(ps[:, j * T + t * P:j * T + (t + 1) * P], sg_v[:, t, h * P:(h + 1) * P],
                                             sg_wm[:, h, :], start=True, stop=True)
                            fill(("mix", i), ins)
                    if (what, n) == ("gate", (1, 0)):
                        ps = open_bank(l, ("mean", 0))
                        pe.wait_ge(conv_step, (l + 1) * KD * CV_TAPS)
                        for k in range(KD):
                            ins = mm(ps[:, 0:T], mean_w[:], y_b[:, k, :], start=(k == 0), stop=(k == KD - 1))
                        fill(("mean", 0), ins)
                        ps = open_bank(l, ("var", 0))
                        pe.wait_ge(cv_squared, l + 1)
                        for k in range(KD):
                            ins = mm(ps[:, 0:T], mean_w[:], cv_sq[:, k, :], start=(k == 0), stop=(k == KD - 1))
                        fill(("var", 0), ins)
                    if what == "ada":
                        ada(l, n)
                    elif what == "in":
                        (token_major if n >= 12 else channel_major)(l, (what, n), u_ch)
                    elif what == "gate":
                        channel_major(l, (what, n), u_ch)
                    elif what == "branch":
                        if n == (0, 0):
                            after_drain(pe, l, ("in", 1, 1))
                        if n == (1, 0):
                            pe.wait_ge(yb_ready, l + 1)
                        if n == (2, 0):
                            pe.wait_ge(yc_ready, (HEADS // 2) * (l + 1))
                        channel_major(l, (what, n), (y_a, y_b, y_c)[n[0]])
                    else:
                        if n == 0:
                            pe.wait_ge(merged_ready, 2 * (KD // MT) * (l + 1))
                        token_major(l, (what, n), merged)
                pe.wait_ge(ln1_done, TT * (l + 1))
                turn(l, "turn2")
                ps = open_bank(l, ("logits", 0))
                for t in range(TT):
                    for k in range(KD):
                        ins = mm(ps[:, t * EXPERTS:(t + 1) * EXPERTS], u_ch[:, k, t * P:(t + 1) * P], router_sb[:, k, :],
                                 start=(k == 0), stop=(k == KD - 1))
                fill(("logits", 0), ins)
                ps = open_bank(l, ("ranks", 0))
                mask = r_small[:, 6]
                pe.wait_ge(mask_ready, l + 1)
                mm(ps[:, 0:EXPERTS], prec[:], mask[:, 0], start=True, stop=True)
                mm(ps[:, EXPERTS:2 * EXPERTS], ones[:], mask[:, 0], start=True, stop=False)
                mm(ps[:, EXPERTS:2 * EXPERTS], prec[:], mask[:, 1], start=False, stop=True)
                mm(ps[:, 2 * EXPERTS:3 * EXPERTS], ones[:], mask[:, 0], start=True, stop=False)
                fill(("ranks", 0), mm(ps[:, 2 * EXPERTS:3 * EXPERTS], ones[:], mask[:, 1], start=False, stop=True))
                for k in range(KD):
                    ps = open_bank(l, ("gather", k))
                    pe.wait_ge(onehot_ready, TT * (l + 1))
                    for t in range(TT):
                        ins = mm(ps[:], x_tok[:, t, k * P:(k + 1) * P], onehot[:, t, :], start=(t == 0), stop=(t == TT - 1))
                    fill(("gather", k), ins)

                pe.wait_ge(blocks_ready, l + 1)
                pe.wait_ge(moe_zeroed, 3 * (l + 1))
                after_drain(pe, l, ("gather", KD - 1))
                after_drain(pe, l, ("gather", KD - 2))
                for t in range(TT):
                    for h in range(2):
                        mm(moe_sum[t][h][:], turned[:, 0:P], y_e, start=True, stop=False, skip_group_check=True)

                def combine(last=False):
                    for t in range(TT):
                        for h in range(2):
                            rows_h = slice(h * BLOCK, (h + 1) * BLOCK)
                            ins = mm(moe_sum[t][h][:], turned[rows_h, 2 * P + t * P:2 * P + (t + 1) * P], y_e[rows_h, :],
                                     start=False, stop=last, skip_group_check=True)
                    return ins

                def expert(l, pair, q):
                    s0 = 3 * q
                    e = 2 * pair + q
                    for i in range(3):
                        s = s0 + i
                        pe.wait_ge(unit_in[s], 16 * (l * PER_SLOT[s] + pair + (MIX[s] + 1)))
                    n = pe.value_load(blocks_i[0:1, bass.ds(e, 1)], min_val=1, max_val=T // BLOCK)
                    with pe.Fori(0, n):
                        b = pe.snap(n_blk)
                        pe.wait_ge(xe_ready, b + 1)
                        for s, ps, ready in ((s0, ps_h1, h1_ready), (s0 + 1, ps_h3, h3_ready)):
                            w = slot(s)
                            for k in range(KD):
                                for h in range(2):
                                    ins = mm(ps[h * BLOCK:(h + 1) * BLOCK, 0:T], xe[:, k, :], w[:, k, h * T:(h + 1) * T],
                                             start=(k == 0), stop=(k == KD - 1))
                            ins.then_inc(ready, 1)
                        pe.wait_ge(y_copied, b)
                        combine()
                        pe.wait_ge(pick_ready, b + 1)
                        for t in range(TT):
                            nc.tensor.transpose(ps_turn[:, 2 * P + t * P:2 * P + (t + 1) * P],
                                                pick[:, t].rearrange("p d s -> p (d s)"), ident[:])
                        pe.wait_ge(hid_ready, b + 1)
                        for c in range(2):
                            ins = nc.tensor.transpose(ps_turn[:, c * P:(c + 1) * P], hid[:, c * P:(c + 1) * P], ident[:])
                        ins.then_inc(turn_ready, 1)
                        pe.wait_ge(turned_ready, b + 1)
                        w = slot(s0 + 2, KE)
                        for f in range(KE):
                            half, c = f // 2, f % 2
                            for h in range(2):
                                ins = mm(ps_y[h * BLOCK:(h + 1) * BLOCK, :],
                                         turned[:, c * P + half * BLOCK:c * P + (half + 1) * BLOCK],
                                         w[:, f, h * HALF:(h + 1) * HALF], start=(f == 0), stop=(f == KE - 1))
                        ins.then_inc(y_ready, 1)
                        pe.reg_add(n_blk, n_blk, 1)

                with pe.Fori(0, MOE_PAIRS) as pair:
                    for q in range(2):
                        expert(l, pair, q)
                pe.wait_ge(y_copied, pe.snap(n_blk))
                combine(True).then_inc(moe_ready, 1)


def kernel(x, c, w_ada, b_ada, w_in, sc_conv, cv_conv, cv_conv_b, cv_ln_g, cv_ln_b, sg_ln_g, sg_ln_b,
           sg_w, sg_b, w_branch, w_gate, b_gate, w_o, ln1_g, ln1_b, w_router, b_router, w1, w3, w2,
           ln2_g, ln2_b):
    import numpy as np
    import concourse.bacc as bacc
    from concourse.bass_utils import run_bass_kernel_spmd

    def cols(a):
        return a.reshape(DEPTH, -1, KD, P).transpose(3, 0, 1, 2)

    ada = b_ada.reshape(DEPTH, 6, D)
    chan = np.concatenate([cols(ada[:, [0, 1, 3, 4]]), cols(sc_conv), cols(cv_conv), cols(cv_conv_b),
                           cols(cv_ln_g), cols(cv_ln_b), cols(b_gate)], axis=2)
    rows = np.stack([sg_ln_g, sg_ln_b, sg_b.reshape(DEPTH, D), ln1_g, ln1_b, ln2_g, ln2_b, ada[:, 2], ada[:, 5]], axis=1)
    i = np.arange(P)
    e = np.arange(EXPERTS)
    consts = np.zeros((P, N_CONST), np.float32)
    consts[:, C_ID:C_ID + P] = np.eye(P)
    consts[:, C_PREC:C_PREC + P] = i[:, None] < i[None, :]
    consts[:, C_TRI16:C_IOTA] = (e[None, :] < e[:, None]).reshape(1, -1)
    consts[:, C_IOTA:] = np.arange(SLOTS)[None, :]
    arrays = {
        "x": x.reshape(T, D), "c_cols": c.reshape(KD, P).T, "w_ada": w_ada, "w_in": w_in, "w_gate": w_gate,
        "w_branch": w_branch, "w_o": w_o, "w1": w1, "w3": w3, "w2": w2, "w_router": w_router,
        "b_router": b_router, "sg_wt": sg_w.transpose(0, 3, 1, 2), "chan": chan, "rows": rows, "consts": consts,
    }
    nc = bacc.Bacc("TRN2", target_bir_lowering=False, num_devices=1)
    feed, args = {}, []
    for name, a in arrays.items():
        a = np.ascontiguousarray(a)
        feed[f"in_{name}"] = a
        args.append(nc.dram_tensor(f"in_{name}", a.shape, mybir.dt.from_np(a.dtype), kind="ExternalInput").ap())
    args.append(nc.dram_tensor("out_x", (T, D), F32, kind="ExternalOutput").ap())
    build(nc, *args)
    result = run_bass_kernel_spmd(nc, [feed], core_ids=[0])
    return result.results[0]["out_x"].reshape(1, T, D)
```

```python
from contextlib import ExitStack

import concourse.bass as bass
from concourse import mybir

F32 = mybir.dt.float32
I32 = mybir.dt.int32
ALU = mybir.AluOpType
ACT = mybir.ActivationFunctionType
AX_X = mybir.AxisListType.X

P = 128
DEPTH = 2
D = 1024
T = 256
TT = T // P
KD = D // P
HALF = D // 2
MT = HALF // P
SC_TAPS, CV_TAPS = 3, 31
HEADS = 8
EXPERTS, GROUPS = 16, 4
PER_GROUP = EXPERTS // GROUPS
TOP_K = 2
DE = 512
KE = DE // P
BLOCK = 64
SLOTS = TOP_K * T
ALPHA = (2.0 * DEPTH) ** 0.25
LN_EPS = 1e-5
PRIMED = 1
BIG = 4096.0

RING = 6
SLOT = KD * HALF
BANKS = 8
BANK = 512

SHIFT1, SCALE1, SHIFT2, SCALE2 = 0, 1, 2, 3
SC_W = 4
CV_W = SC_W + SC_TAPS
CV_B = CV_W + CV_TAPS
CV_G, CV_LB = CV_B + 1, CV_B + 2
B_GATE = CV_B + 3
N_CHAN = B_GATE + 3
ROW_SG, ROW_LN1, ROW_LN2, ROW_GATE = 0, 3, 5, 7
N_ROWS = 9
C_ID, C_PREC = 0, P
C_TRI16 = 2 * P
C_IOTA = C_TRI16 + EXPERTS * EXPERTS
N_CONST = C_IOTA + SLOTS

ADA_PARTS = [0, 0, 1, 1, 2, 2, 3, 3, 4, 4, 5, 5]
NEXT = 4
UNITS = [("in", 8), ("in", 6), ("in", 9), ("in", 7),
         ("in", 12), ("in", 13), ("ada", 4), ("in", 2), ("ada", 5), ("in", 4),
         ("in", 3), ("in", 5), ("in", 0), ("ada", 6), ("in", 1), ("ada", 7),
         ("in", 10), ("ada", 8), ("in", 11), ("ada", 9),
         ("gate", (0, 0)), ("ada", 10), ("gate", (0, 1)), ("ada", 11), ("gate", (2, 0)), ("gate", (2, 1)),
         ("branch", (0, 0)), ("branch", (0, 1)), ("ada", 0), ("ada", 1), ("gate", (1, 0)), ("gate", (1, 1)),
         ("branch", (2, 0)), ("branch", (2, 1)), ("ada", 2), ("ada", 3), ("branch", (1, 0)), ("branch", (1, 1)),
         ("o", 0), ("o", 1)]
PE_ORDER = [("in", 8), ("in", 6), ("in", 9), ("in", 7), ("in", 12), ("in", 13), ("in", 2), ("in", 4), ("in", 3),
            ("ada", 4), ("ada", 5), ("in", 5), ("in", 0), ("in", 1), ("in", 10), ("in", 11), ("mean", 0),
            ("ada", 6), ("ada", 7), ("mix", 0), ("gate", (0, 0)), ("var", 0), ("gate", (0, 1)), ("ada", 8), ("ada", 9),
            ("gate", (2, 0)), ("gate", (2, 1)), ("ada", 10), ("ada", 11), ("branch", (0, 0)), ("branch", (0, 1)),
            ("gate", (1, 0)), ("ada", 0), ("ada", 1), ("gate", (1, 1)), ("branch", (2, 0)), ("branch", (2, 1)),
            ("branch", (1, 0)), ("ada", 2), ("ada", 3), ("branch", (1, 1)), ("o", 0), ("o", 1)]
ADA_ORDER = [n for what, n in PE_ORDER if what == "ada"]
UNIT = {u: i for i, u in enumerate(UNITS)}
MIX = [len(range(s, len(UNITS), RING)) for s in range(RING)]
MOE_PAIRS = EXPERTS // 2
PER_SLOT = [m + MOE_PAIRS for m in MIX]


def bank_uses():
    by_act = {8, 9, 12, 13, 2, 3, 10, 11}
    uses = [(("turn1", i), "act" if i % 2 == 0 else "dve") for i in range(KD // 2)]
    for what, n in PE_ORDER:
        if what == "mix":
            uses += [(("mix", i), "dve") for i in range(HEADS // 2)]
        elif what in ("mean", "ada"):
            uses.append(((what, n), "dve"))
        elif what == "var":
            uses.append(((what, n), "act"))
        else:
            who = "act" if what == "gate" or (what == "in" and n in by_act) else "dve"
            uses += [((what, n, i), who) for i in range(2)]
    uses += [(("turn2", i), "act" if i % 2 == 0 else "dve") for i in range(KD // 2)]
    uses += [(("logits", 0), "dve"), (("ranks", 0), "dve")]
    uses += [(("gather", i), "act" if i % 2 == 0 else "dve") for i in range(KD)]
    return uses


USES = bank_uses()
USE = {what: i for i, (what, _) in enumerate(USES)}
N_USES = len(USES)
N_DRAINED = {e: sum(w == e for _, w in USES) for e in ("act", "dve")}
DRAINED = {what: (e, sum(w == e for _, w in USES[:i + 1])) for i, (what, e) in enumerate(USES)}
DVE_CHAIN = 186


def build(nc, x, c_cols, w_ada, w_in, w_gate, w_branch, w_o, w1, w3, w2, w_router, b_router,
          sg_wt, chan, rows, consts, out):
    ctx = ExitStack()
    with ctx:
        def sb(name, shape, dt=F32):
            return ctx.enter_context(nc.sbuf_tensor(name, shape, dt))

        def sem(name):
            return ctx.enter_context(nc.semaphore(name))

        ring = sb("ring", [P, RING, SLOT])
        x_tok = sb("x_tok", [P, TT, D])
        u_ch = sb("u_ch", [P, KD, T])
        row_buf = sb("row_buf", [P, 3, D])
        gate_row = sb("gate_row", [P, 2, D])
        chan_sb = sb("chan_sb", [P, DEPTH, N_CHAN, KD])
        mod = sb("mod", [P, 4, KD])
        c_act = sb("c_act", [P, KD])
        ada_sum = sb("ada_sum", [P, 2, HALF])
        ones = sb("ones", [P, P])
        mean_w = sb("mean_w", [P, P])
        ident = sb("ident", [P, P])
        prec = sb("prec", [P, P])
        router_sb = sb("router_sb", [P, KD, EXPERTS])
        brout_sb = sb("brout_sb", [P, EXPERTS])
        eps = sb("eps", [P, 1])
        stats = sb("stats", [P, TT, 2, 6])
        aggr = sb("aggr", [P, TT, 2])
        std = sb("std", [P, TT])
        rstd = sb("rstd", [P, TT])
        blocks_i = sb("blocks_i", [1, EXPERTS], I32)
        start_i = sb("start_i", [1, EXPERTS], I32)
        CV_PAD = CV_TAPS - 1
        SC_PAD = SC_TAPS - 1
        cv_in_n, sc_in_n, full = KD * (T + CV_PAD), KD * (T + SC_PAD), KD * T
        shared_n = 5 * full + cv_in_n + sc_in_n + 2 * BANK + HEADS * P
        shared = sb("shared", [P, shared_n])
        at = [0]

        def part(n):
            at[0] += n
            return shared[:, at[0] - n:at[0]]

        gate_a = part(full).rearrange("p (k t) -> p k t", k=KD)
        sc_part = part(sc_in_n)
        sc_in = sc_part.rearrange("p (k t) -> p k t", k=KD)
        gate_b = sc_part[:, 0:full].rearrange("p (k t) -> p k t", k=KD)
        y_a = part(full).rearrange("p (k t) -> p k t", k=KD)
        cv_part = part(cv_in_n)
        cv_in = cv_part.rearrange("p (k t) -> p k t", k=KD)
        cv_sq = cv_part[:, 0:full].rearrange("p (k t) -> p k t", k=KD)
        y_b = part(full).rearrange("p (k t) -> p k t", k=KD)
        y_c = part(full).rearrange("p (k t) -> p k t", k=KD)
        sg_flat = part(full)
        sg_v = sg_flat.rearrange("p (n c) -> p n c", n=TT)
        merged = sg_flat.rearrange("p (k t) -> p k t", k=KD)
        tmp = part(2 * BANK).rearrange("p (b n) -> p b n", b=2)
        sg_wm = part(HEADS * P).rearrange("p (h t) -> p h t", h=HEADS)
        glu_sig = gate_a
        cv_mean, cv_std, cv_rstd = (cv_part[:, i * T:(i + 1) * T] for i in range(3))

        at[0] = 0
        SORTED = SLOTS + BLOCK
        sorted_ch = part(KD * SORTED).rearrange("p (k s) -> p k s", k=KD)
        onehot = part(TT * SLOTS).rearrange("p (n s) -> p n s", n=TT)
        iota = part(SLOTS)
        tri16 = part(EXPERTS * EXPERTS).rearrange("p (a b) -> p a b", a=EXPERTS)
        xe = part(KD * BLOCK).rearrange("p (k s) -> p k s", k=KD)
        silu_e = part(T)
        hid = part(T)
        turned = part(BANK)
        y_two = part(D)
        pick = part(2 * TT * P).rearrange("p (q n s) -> p q n s", q=2, n=TT)
        r_small = part(24 * TT * EXPERTS).rearrange("p (v n e) -> p v n e", v=24, n=TT)
        r_wide = part(3 * EXPERTS * EXPERTS).rearrange("p (v n) -> p v n", v=3)
        assert at[0] <= shared_n

        psum = [ctx.enter_context(nc.psum_tensor(f"bank{b}", [P, BANK], F32)) for b in range(BANKS)]
        moe_sum = [[psum[2 * n + h] for h in range(2)] for n in range(TT)]
        ps_h1, ps_h3, ps_turn, ps_y = psum[4], psum[5], psum[6], psum[7]

        params_in = sem("params_in")
        consts_ready = sem("consts_ready")
        c_ready = sem("c_ready")
        unit_in = [sem(f"unit_in{s}") for s in range(RING)]
        bank_full = sem("bank_full")
        drained = {"act": sem("act_drained"), "dve": sem("dve_drained")}
        chain = sem("chain")
        first_chain = sem("first_chain")
        ada_ready = sem("ada_ready")
        conv_step = sem("conv_step")
        rows_in, gates_in, sgw_in, moe_consts_in = sem("rows_in"), sem("gates_in"), sem("sgw_in"), sem("moe_consts_in")
        pads_ready = sem("pads_ready")
        sgw_masked = sem("sgw_masked")
        sgv_ready = sem("sgv_ready")
        ln_var, ln_std = sem("ln_var"), sem("ln_std")
        ln1_done = sem("ln1_done")
        yc_ready = sem("yc_ready")
        cv_ready, cv_centred, cv_squared, cv_normed, yb_ready = (
            sem("cv_ready"), sem("cv_centred"), sem("cv_squared"), sem("cv_normed"), sem("yb_ready"))
        merged_ready = sem("merged_ready")
        max_ready, exp_ready = sem("max_ready"), sem("exp_ready")
        mask_ready, onehot_ready, blocks_ready = sem("mask_ready"), sem("onehot_ready"), sem("blocks_ready")
        moe_zeroed, pos_step = sem("moe_zeroed"), sem("pos_step")
        xe_ready, pick_ready = sem("xe_ready"), sem("pick_ready")
        h1_ready, h3_ready, silu_ready, hid_ready = sem("h1_ready"), sem("h3_ready"), sem("silu_ready"), sem("hid_ready")
        turn_ready, turned_ready, y_ready, y_copied = sem("turn_ready"), sem("turned_ready"), sem("y_ready"), sem("y_copied")
        moe_ready, ln2_done, out_done = sem("moe_ready"), sem("ln2_done"), sem("out_done")

        passed = {e: sem(f"passed_{e}") for e in ("SP", "Pool", "DVE")}

        ada_v = w_ada.rearrange("l (k p) n -> l p k n", p=P)
        in_v = w_in.rearrange("l (k p) n -> l p k n", p=P)
        gate_v = w_gate.rearrange("l (k p) b n -> l p k b n", p=P)
        branch_v = w_branch.rearrange("l b (k p) n -> l b p k n", p=P)
        o_v = w_o.rearrange("l (k p) n -> l p k n", p=P)
        w1_v = w1.rearrange("l e (k p) f -> l e p k f", p=P)
        w3_v = w3.rearrange("l e (k p) f -> l e p k f", p=P)
        w2_v = w2.rearrange("l e (k p) n -> l e p k n", p=P)

        def slot(s, k=KD):
            return ring[:, s, :].rearrange("p (k n) -> p k n", k=k)

        def unit_dram(u, l):
            what, n = UNITS[u]
            cols = lambda i: slice(i * HALF, (i + 1) * HALF)
            if what == "ada":
                if n < NEXT:
                    return ada_v[(l + 1) % DEPTH][:, :, cols(n)]
                return ada_v[l][:, :, cols(n)]
            if what == "in":
                return in_v[l][:, :, cols(n)]
            if what == "gate":
                return gate_v[l][:, :, n[0], cols(n[1])]
            if what == "branch":
                return branch_v[l, n[0]][:, :, cols(n[1])]
            return o_v[l][:, :, cols(n)]

        def alone(eng):
            eng.sem_inc(passed[eng.engine.name], 1)

        def unit_loaded(eng, l, u):
            eng.wait_ge(unit_in[u % RING], 16 * (l * PER_SLOT[u % RING] + (u // RING + 1 + (u % RING < NEXT))))

        def ada_summed(eng, l, n):
            eng.wait_ge(ada_ready, len(ADA_PARTS) * l + (NEXT + ADA_ORDER.index(n) + 1))

        def unit_read(eng, l, u):
            what, n = UNITS[u]
            if what == "ada":
                ada_summed(eng, l, n)
            else:
                filled(eng, l, (what, n, 1))

        def filled(eng, l, what):
            eng.wait_ge(bank_full, l * N_USES + (NEXT + USE[what] + 1))

        def after_drain(eng, l, what):
            who, n = DRAINED[what]
            eng.wait_ge(drained[who], l * N_DRAINED[who] + (n + (NEXT if who == "dve" else 0)))

        def bank(what):
            return psum[USE[what] % BANKS]

        block = ctx.enter_context(nc.Block())

        @block.sync
        def _(sp):
            sp.dma_start(c_act[:], c_cols).then_inc(params_in, 16)
            sp.dma_start(x_tok[:], x.rearrange("(n p) d -> p n d", p=P)).then_inc(params_in, 16)
            sp.dma_start(ident[:], consts[:, C_ID:C_ID + P]).then_inc(params_in, 16)
            sp.dma_start(chan_sb[:], chan).then_inc(params_in, 16)
            sp.dma_start(prec[:], consts[:, C_PREC:C_PREC + P]).then_inc(params_in, 16)
            sp.dma_start(router_sb[:], w_router.rearrange("(k p) e -> p k e", p=P)).then_inc(params_in, 16)
            sp.dma_start(brout_sb[:], b_router.partition_broadcast(P)).then_inc(params_in, 16)
            done = sp.alloc_register("blocks_done")
            sp.reg_mov(done, PRIMED)
            for n in range(NEXT):
                sp.dma_start(slot(n), ada_v[0][:, :, n * HALF:(n + 1) * HALF]).then_inc(unit_in[n], 16)
            with sp.Fori(0, DEPTH) as l:
                for u in range(len(UNITS)):
                    if u < NEXT:
                        sp.wait_ge(ada_ready, len(ADA_PARTS) * l + u + 1)
                        alone(sp)
                    if u < RING:
                        sp.wait_ge(y_ready, sp.snap(done))
                    else:
                        unit_read(sp, l, u - RING)
                    alone(sp)
                    sp.dma_start(slot(u % RING), unit_dram(u, l)).then_inc(unit_in[u % RING], 16)

                def expert(e, s0, wait):
                    for i, (src, k) in enumerate(((w1_v, KD), (w3_v, KD), (w2_v, KE))):
                        wait(s0 + i, (h1_ready, h3_ready, y_ready)[i])
                        alone(sp)
                        sp.dma_start(slot(s0 + i, k), src[l, e]).then_inc(unit_in[s0 + i], 16)

                for e in range(2):
                    expert(e, 3 * e, lambda s, _: unit_read(sp, l, max(range(s, len(UNITS), RING))))
                sp.wait_ge(blocks_ready, l + 1)
                alone(sp)
                with sp.Fori(1, MOE_PAIRS) as pair:
                    for q in range(2):
                        n = sp.value_load(blocks_i[0:1, bass.ds(2 * pair + (q - 2), 1)], min_val=1, max_val=T // BLOCK)
                        sp.reg_add(done, done, n)
                        expert(2 * pair + q, 3 * q, lambda _, last_read: sp.wait_ge(last_read, sp.snap(done)))
                for e in (EXPERTS - 2, EXPERTS - 1):
                    n = sp.value_load(blocks_i[0:1, e:e + 1], min_val=1, max_val=T // BLOCK)
                    sp.reg_add(done, done, n)
            sp.wait_ge(ln2_done, DEPTH * TT + PRIMED)
            sp.dma_start(out.rearrange("(n p) d -> p n d", p=P), x_tok[:]).then_inc(out_done, 16)
            sp.wait_ge(out_done, 16)

        @block.gpsimd
        def _(pool):
            nc.gpsimd.memset(ones[:], 1.0).then_inc(consts_ready, 1)
            nc.gpsimd.memset(mean_w[:], 1.0 / D).then_inc(consts_ready, 1)
            nc.gpsimd.memset(eps[:], LN_EPS).then_inc(consts_ready, 1)
            with pool.Fori(0, DEPTH) as l:
                pool.wait_ge(ln2_done, l * TT + PRIMED)
                pool.dma_start(row_buf[:, 0:3, :], rows[l, ROW_SG:ROW_SG + 3].partition_broadcast(P)).then_inc(rows_in, 16)
                pool.dma_start(gate_row[:, :, :], rows[l, ROW_GATE:ROW_GATE + 2].partition_broadcast(P)).then_inc(gates_in, 16)
                pool.dma_start(sg_wm, sg_wt[l]).then_inc(sgw_in, 16)
                nc.gpsimd.memset(cv_in[:, :, 0:CV_PAD], 0.0).then_inc(pads_ready, 1)
                nc.gpsimd.memset(sc_in[:, :, 0:SC_PAD], 0.0).then_inc(pads_ready, 1)
                pool.wait_ge(sgw_in, 16 * (l + 1))
                alone(pool)
                nc.gpsimd.affine_select(out=sg_wm, in_=sg_wm, compare_op=ALU.is_ge, fill=0.0, base=0,
                                        pattern=[[0, HEADS], [1, P]], channel_multiplier=-1).then_inc(sgw_masked, 1)
                pool.wait_ge(yc_ready, (HEADS // 2) * (l + 1))
                pool.dma_start(row_buf[:, 0:2, :], rows[l, ROW_LN1:ROW_LN1 + 2].partition_broadcast(P)).then_inc(rows_in, 16)
                pool.wait_ge(ln1_done, TT * (l + 1))
                pool.dma_start(row_buf[:, 0:2, :], rows[l, ROW_LN2:ROW_LN2 + 2].partition_broadcast(P)).then_inc(rows_in, 16)
                pool.dma_start(iota, consts[:, C_IOTA:C_IOTA + SLOTS]).then_inc(moe_consts_in, 16)
                pool.dma_start(tri16, consts[:, C_TRI16:C_IOTA].rearrange("p (a b) -> p a b", a=EXPERTS)).then_inc(moe_consts_in, 16)
                nc.gpsimd.memset(sorted_ch[:, :, SLOTS:SORTED], 0.0).then_inc(moe_zeroed, 1)
                nc.gpsimd.memset(y_two, 0.0).then_inc(moe_zeroed, 1)
                nc.gpsimd.memset(turned, 0.0).then_inc(moe_zeroed, 1)
                nc.gpsimd.memset(pick, 0.0).then_inc(moe_zeroed, 1)

        @block.scalar
        def _(act):
            act.wait_ge(params_in, 16 * 7)
            nc.scalar.activation(c_act[:], c_act[:], ACT.Silu).then_inc(c_ready, 1)
            act.wait_ge(consts_ready, 3)
            n_blk = act.alloc_register("act_block")
            act.reg_mov(n_blk, PRIMED)
            act.sem_inc(silu_ready, PRIMED)
            act.sem_inc(turned_ready, PRIMED)
            act.sem_inc(y_copied, PRIMED)

            def turn(l, name, which, shift, scale):
                for i in range(0, KD // 2, 2):
                    filled(act, l, (name, i))
                    for j in range(2):
                        k = 2 * i + j
                        ins = nc.scalar.activation(u_ch[:, k, :], bank((name, i))[:, j * T:(j + 1) * T], ACT.Identity,
                                                   bias=mod[:, shift, k:k + 1], scale=mod[:, scale, k:k + 1])
                    ins.then_inc(drained["act"], 1)

            def pairs(l, unit, dst, func):
                for i in range(2):
                    filled(act, l, (*unit, i))
                    nc.scalar.activation(dst(i), bank((*unit, i))[:], func).then_inc(drained["act"], 1)

            def two(buf, col, i):
                k = MT * col + 2 * i
                return buf[:, k:k + 2, :].rearrange("p k t -> p (k t)")

            def gates(l, b, dst, col):
                for i in range(2):
                    filled(act, l, ("gate", (b, col), i))
                    for j in range(2):
                        k = MT * col + 2 * i + j
                        ins = nc.scalar.activation(dst[:, k, :], bank(("gate", (b, col), i))[:, j * T:(j + 1) * T],
                                                   ACT.Sigmoid, bias=chan_at(l, B_GATE + b, k))
                    ins.then_inc(drained["act"], 1)

            def chan_at(l, v, k):
                return chan_sb[:, bass.ds(l, 1), v, k:k + 1].rearrange("p a b -> p (a b)")

            def deviation(l, n):
                act.wait_ge(ln_var, 3 * l + n + 1)
                nc.scalar.activation(std[:], aggr[:, :, 1], ACT.Sqrt, bias=eps[:, 0:1]).then_inc(ln_std, 1)

            with act.Fori(0, DEPTH) as l:
                turn(l, "turn1", 0, SHIFT1, SCALE1)
                pairs(l, ("in", 8), lambda i: two(glu_sig, 0, i), ACT.Sigmoid)
                pairs(l, ("in", 9), lambda i: two(glu_sig, 1, i), ACT.Sigmoid)
                for h in range(2):
                    pairs(l, ("in", 12 + h), lambda i: sg_v[:, i, h * HALF:(h + 1) * HALF], ACT.Gelu_apprx_tanh)
                deviation(l, 0)
                for col in range(2):
                    pairs(l, ("in", 2 + col), lambda i: two(y_a, col, i), ACT.Copy)
                for col in range(2):
                    pairs(l, ("in", 10 + col), lambda i: two(y_c, col, i), ACT.Gelu_apprx_tanh)
                act.wait_ge(cv_centred, l + 1)
                nc.scalar.activation(cv_sq, y_b, ACT.Square).then_inc(cv_squared, 1)
                gates(l, 0, gate_a, 0)
                filled(act, l, ("var", 0))
                nc.scalar.activation(cv_std, bank(("var", 0))[:, 0:T], ACT.Sqrt, bias=eps[:, 0:1]).then_inc(drained["act"], 1)
                gates(l, 0, gate_a, 1)
                after_drain(act, l, ("in", 1, 1))
                gates(l, 2, gate_b, 0)
                gates(l, 2, gate_b, 1)
                act.wait_ge(cv_normed, l + 1)
                for k in range(KD):
                    ins = nc.scalar.activation(y_b[:, k, :], y_b[:, k, :], ACT.Silu, bias=chan_at(l, CV_LB, k),
                                               scale=chan_at(l, CV_G, k))
                ins.then_inc(yb_ready, 1)
                after_drain(act, l, ("branch", (0, 1), 1))
                gates(l, 1, gate_a, 0)
                gates(l, 1, gate_a, 1)
                deviation(l, 1)
                turn(l, "turn2", 0, SHIFT2, SCALE2)
                act.wait_ge(max_ready, l + 1)
                nc.scalar.activation(r_small[:, 1], r_small[:, 0], ACT.Exp).then_inc(exp_ready, 1)
                for k in range(0, KD, 2):
                    filled(act, l, ("gather", k))
                    nc.scalar.activation(sorted_ch[:, k, 0:SLOTS], bank(("gather", k))[:], ACT.Identity,
                                         bias=mod[:, SHIFT2, k:k + 1],
                                         scale=mod[:, SCALE2, k:k + 1]).then_inc(drained["act"], 1)
                act.wait_ge(blocks_ready, l + 1)
                act.wait_ge(moe_zeroed, 4 * (l + 1))

                def expert(pair, q):
                    e = 2 * pair + q
                    n = act.value_load(blocks_i[0:1, bass.ds(e, 1)], min_val=1, max_val=T // BLOCK)
                    with act.Fori(0, n):
                        b = act.snap(n_blk)
                        act.wait_ge(h1_ready, b + 1)
                        nc.scalar.activation(silu_e, ps_h1[:, 0:T], ACT.Silu).then_inc(silu_ready, 1)
                        act.wait_ge(turn_ready, b + 1)
                        nc.scalar.activation(turned, ps_turn[:], ACT.Copy).then_inc(turned_ready, 1)
                        act.wait_ge(y_ready, b + 1)
                        for h in range(2):
                            ins = nc.scalar.activation(y_two[q * BLOCK:(q + 1) * BLOCK, h * HALF:(h + 1) * HALF],
                                                       ps_y[h * BLOCK:(h + 1) * BLOCK, :], ACT.Copy)
                        ins.then_inc(y_copied, 1)
                        act.reg_add(n_blk, n_blk, 1)

                with act.Fori(0, MOE_PAIRS) as pair:
                    for q in range(2):
                        expert(pair, q)
                deviation(l, 2)

        @block.vector
        def _(dve):
            v = nc.vector
            steps = [0]
            n_blk = dve.alloc_register("dve_block")
            dve.reg_mov(n_blk, PRIMED)
            dve.sem_inc(xe_ready, PRIMED)
            dve.sem_inc(pick_ready, PRIMED)
            dve.sem_inc(hid_ready, PRIMED)
            dve.sem_inc(ln2_done, PRIMED)

            def chan_at(l, n, k):
                return chan_sb[:, bass.ds(l, 1), n, k:k + 1].rearrange("p a b -> p (a b)")

            def then(l, ins):
                steps[0] += 1
                ins.then_inc(chain, 1)
                dve.wait_ge(chain, l * DVE_CHAIN + steps[0])

            def drain(ins):
                ins.then_inc(drained["dve"], 1)

            first_steps = [0]

            def link_first(ins):
                first_steps[0] += 1
                ins.then_inc(first_chain, 1)
                dve.wait_ge(first_chain, first_steps[0])

            def ada_sums(l, n, w, before, link):
                acc = ada_sum[:, n % 2, :]
                before()
                link(v.tensor_scalar(acc, w[:, 0, :], c_act[:, 0:1], None, ALU.mult))
                for k in range(1, KD):
                    ins = v.scalar_tensor_tensor(out=acc, in0=w[:, k, :], scalar=c_act[:, k:k + 1], in1=acc,
                                                 op0=ALU.mult, op1=ALU.add)
                    if k < KD - 1:
                        link(ins)
                ins.then_inc(ada_ready, 1)

            def ada_unit(l, n):
                u = UNIT[("ada", n)]
                unit_loaded(dve, l, u)
                i = ADA_ORDER.index(n)
                ada_sums(l, n, slot(u % RING), lambda: filled(dve, l, ("ada", ADA_ORDER[i - 2])) if i >= 2 else None,
                         lambda ins: then(l, ins))

            def ada_store(l, n, ps):
                part, half = ADA_PARTS[n], n % 2
                if part in (2, 5):
                    row = gate_row[:, part // 5, half * HALF:(half + 1) * HALF]
                    return v.tensor_tensor(row, ps[:], row, ALU.add)
                m = {0: SHIFT1, 1: SCALE1, 3: SHIFT2, 4: SCALE2}[part]
                b = chan_sb[:, bass.ds(l, 1), m, half * MT:(half + 1) * MT].rearrange("p a b -> p (a b)")
                return v.scalar_tensor_tensor(out=mod[:, m, half * MT:(half + 1) * MT], in0=ps[:, 0:MT],
                                              scalar=1.0 if part in (1, 4) else 0.0, in1=b,
                                              op0=ALU.add, op1=ALU.add)

            def ada_out(l, n):
                filled(dve, l, ("ada", n))
                if ADA_PARTS[n] in (2, 5):
                    dve.wait_ge(gates_in, 16 * (l + 1))
                drain(ada_store((l + 1) % DEPTH if n < NEXT else l, n, bank(("ada", n))))

            def turn(l, name, shift, scale):
                for i in range(1, KD // 2, 2):
                    filled(dve, l, (name, i))
                    for j in range(2):
                        k = 2 * i + j
                        ins = v.tensor_scalar(u_ch[:, k, :], bank((name, i))[:, j * T:(j + 1) * T],
                                              mod[:, scale, k:k + 1], mod[:, shift, k:k + 1], ALU.mult, ALU.add)
                    drain(ins)

            def conv31(l, pair, nth):
                tiles = (2 * pair, 2 * pair + 1)
                base = l * (KD * CV_TAPS) + 2 * nth * CV_TAPS

                def step(j, a, at):
                    k = tiles[a]
                    if isinstance(j, int) and j == 0:
                        return v.tensor_scalar(y_b[:, k, :], cv_in[:, k, 0:T], chan_at(l, CV_W, k),
                                               chan_at(l, CV_B, k), ALU.mult, ALU.add).then_inc(conv_step, 1)
                    w = chan_sb[:, bass.ds(l, 1), bass.ds(j + CV_W, 1), k:k + 1].rearrange("p a b c -> p (a b c)")
                    dve.wait_ge(conv_step, at)
                    return v.scalar_tensor_tensor(out=y_b[:, k, :], in0=cv_in[:, k, bass.ds(j, T)], scalar=w,
                                                  in1=y_b[:, k, :], op0=ALU.mult, op1=ALU.add).then_inc(conv_step, 1)

                for a in range(2):
                    step(0, a, 0)
                unroll = 5
                with dve.Fori(0, (CV_TAPS - 1) // unroll) as r:
                    for i in range(unroll):
                        for a in range(2):
                            step(r * unroll + (i + 1), a, base + 2 * unroll * r + (2 * i + a + 1))

            def conv3(l, pair):
                for a in range(2):
                    k = 2 * pair + a
                    v.tensor_scalar(y_a[:, k, :], sc_in[:, k, 0:T], chan_at(l, SC_W, k), None,
                                    ALU.mult).then_inc(chain, 1)
                steps[0] += 2
                dve.wait_ge(chain, l * DVE_CHAIN + steps[0])
                for j in range(1, SC_TAPS):
                    for a in range(2):
                        k = 2 * pair + a
                        v.scalar_tensor_tensor(out=y_a[:, k, :], in0=sc_in[:, k, j:j + T],
                                               scalar=chan_at(l, SC_W + j, k), in1=y_a[:, k, :],
                                               op0=ALU.mult, op1=ALU.add).then_inc(chain, 1)
                    steps[0] += 2
                    dve.wait_ge(chain, l * DVE_CHAIN + steps[0])

            def flat(buf, col, i):
                k = MT * col + 2 * i
                return buf[:, k:k + 2, :]

            def ps2(what):
                return bank(what)[:].rearrange("p (k t) -> p k t", k=2)

            def norm_rows(l, n, buf, row_in, signal, gain=0):
                alone(dve)
                for t in range(TT):
                    ins = v.bn_aggr(aggr[:, t, :], stats[:, t].rearrange("p h s -> p (h s)"))
                ins.then_inc(ln_var, 1)
                dve.wait_ge(ln_std, 3 * l + n + 1)
                then(l, v.reciprocal(rstd[:], std[:]))
                dve.wait_ge(rows_in, row_in)
                for t in range(TT):
                    then(l, v.tensor_scalar(buf[:, t, :], buf[:, t, :], aggr[:, t, 0:1], rstd[:, t:t + 1],
                                            ALU.subtract, ALU.mult))
                    then(l, v.tensor_tensor(buf[:, t, :], buf[:, t, :], row_buf[:, 0, :], ALU.mult))
                    v.tensor_tensor(buf[:, t, :], buf[:, t, :], row_buf[:, 1, :], ALU.add).then_inc(signal, 1)

            def residual(l, ps, gate, t, h):
                xs = x_tok[:, t, h * HALF:(h + 1) * HALF]
                v.tensor_tensor(tmp[:, 0, :], ps[:], gate_row[:, gate, h * HALF:(h + 1) * HALF], ALU.mult).then_inc(chain, 1)
                steps[0] += 1
                dve.wait_ge(chain, l * DVE_CHAIN + steps[0])
                then(l, v.scalar_tensor_tensor(out=xs, in0=xs, scalar=ALPHA, in1=tmp[:, 0, :],
                                               op0=ALU.mult, op1=ALU.add))
                return v.bn_stats(stats[:, t, h, :], xs)

            dve.wait_ge(params_in, 16 * 7)
            dve.wait_ge(c_ready, 1)
            for n in range(NEXT):
                dve.wait_ge(unit_in[n], 16)
                ada_sums(0, n, slot(n), lambda: dve.wait_ge(bank_full, n - 1) if n >= 2 else None, link_first)
                if n:
                    dve.wait_ge(bank_full, n)
                    drain(ada_store(0, n - 1, psum[n - 1]))
            dve.wait_ge(bank_full, NEXT)
            drain(ada_store(0, NEXT - 1, psum[NEXT - 1]))
            dve.wait_ge(drained["dve"], NEXT)
            with dve.Fori(0, DEPTH) as l:
                steps[0] = 0
                turn(l, "turn1", SHIFT1, SCALE1)

                dve.wait_ge(pads_ready, 2 * (l + 1))
                for col in range(2):
                    after_drain(dve, l, ("in", 8 + col, 1))
                    for i in range(2):
                        what = ("in", 6 + col, i)
                        filled(dve, l, what)
                        k = MT * col + 2 * i
                        drain(v.tensor_tensor(cv_in[:, k:k + 2, CV_PAD:CV_PAD + T], ps2(what), flat(glu_sig, col, i), ALU.mult))
                    after_drain(dve, l, ("in", 6 + col, 1))
                    conv31(l, 2 * col, col)

                after_drain(dve, l, ("in", 13, 1))
                for t in range(TT):
                    for h in range(2):
                        ins = v.bn_stats(stats[:, t, h, :], sg_v[:, t, h * HALF:(h + 1) * HALF])
                then(l, ins)
                norm_rows(l, 0, sg_v, 48 * l + 16, sgv_ready)
                ada_unit(l, 4)
                ada_unit(l, 5)

                for col in range(2):
                    after_drain(dve, l, ("in", 2 + col, 1))
                    for i in range(2):
                        what = ("in", 4 + col, i)
                        filled(dve, l, what)
                        k = MT * col + 2 * i
                        drain(v.tensor_tensor(sc_in[:, k:k + 2, SC_PAD:SC_PAD + T], ps2(what), flat(y_a, col, i), ALU.mult))
                    after_drain(dve, l, ("in", 4 + col, 1))
                    conv31(l, 2 * col + 1, 2 + col)
                    for i in range(2):
                        conv3(l, 2 * col + i)
                    if col == 0:
                        ada_out(l, 4)
                        ada_out(l, 5)
                for col in range(2):
                    for i in range(2):
                        what = ("in", col, i)
                        filled(dve, l, what)
                        drain(v.tensor_tensor(flat(y_a, col, i), ps2(what), flat(y_a, col, i), ALU.mult))
                ada_unit(l, 6)
                ada_unit(l, 7)

                filled(dve, l, ("mean", 0))
                drain(v.tensor_copy(cv_mean, bank(("mean", 0))[:, 0:T]))
                after_drain(dve, l, ("mean", 0))
                v.tensor_tensor(y_b, y_b, cv_mean.unsqueeze(1).broadcast_to([P, KD, T]), ALU.subtract).then_inc(cv_centred, 1)
                ada_out(l, 6)
                ada_out(l, 7)
                ada_unit(l, 8)
                after_drain(dve, l, ("in", 11, 1))
                for i in range(HEADS // 2):
                    what = ("mix", i)
                    filled(dve, l, what)
                    if i >= 2:
                        dve.wait_ge(yc_ready, (HEADS // 2) * l + i - 1)
                    srow = row_buf[:, 2, :].rearrange("p (h t) -> p h t", h=HEADS)
                    o4 = tmp[:, i % 2, :].rearrange("p (h n t) -> p h n t", h=2, n=TT)
                    drain(v.tensor_tensor(o4, bank(what)[:].rearrange("p (h n t) -> p h n t", h=2, n=TT),
                                          srow[:, 2 * i:2 * i + 2, :].unsqueeze(2).broadcast_to([P, 2, TT, P]), ALU.add))
                    after_drain(dve, l, what)
                    yc = y_c[:, 2 * i:2 * i + 2, :].rearrange("p k t -> p (k t)")
                    v.tensor_tensor(yc, yc, tmp[:, i % 2, :], ALU.mult).then_inc(yc_ready, 1)
                ada_unit(l, 9)
                after_drain(dve, l, ("var", 0))
                then(l, v.reciprocal(cv_rstd, cv_std))
                v.tensor_tensor(y_b, y_b, cv_rstd.unsqueeze(1).broadcast_to([P, KD, T]), ALU.mult).then_inc(cv_normed, 1)
                ada_out(l, 8)
                ada_out(l, 9)
                ada_unit(l, 10)
                ada_unit(l, 11)
                ada_out(l, 10)
                ada_out(l, 11)

                def branch(b, gate, col, first=False):
                    after_drain(dve, l, ("gate", (b, col), 1))
                    for i in range(2):
                        what = ("branch", (b, col), i)
                        filled(dve, l, what)
                        if first:
                            drain(v.tensor_tensor(flat(merged, col, i), ps2(what), flat(gate, col, i), ALU.mult))
                        else:
                            t2 = tmp[:, i, :].rearrange("p (k t) -> p k t", k=2)
                            drain(v.tensor_tensor(t2, ps2(what), flat(gate, col, i), ALU.mult))
                            after_drain(dve, l, what)
                            ins = v.tensor_tensor(flat(merged, col, i), flat(merged, col, i), t2, ALU.add)
                            if b == 1:
                                ins.then_inc(merged_ready, 1)
                            else:
                                then(l, ins)

                for col in range(2):
                    branch(0, gate_a, col, True)
                ada_unit(l, 0)
                ada_unit(l, 1)
                ada_out(l, 0)
                ada_out(l, 1)
                for col in range(2):
                    branch(2, gate_b, col)
                ada_unit(l, 2)
                ada_unit(l, 3)
                branch(1, gate_a, 0)
                ada_out(l, 2)
                ada_out(l, 3)
                branch(1, gate_a, 1)

                for h in range(2):
                    for t in range(TT):
                        filled(dve, l, ("o", h, t))
                        drain(residual(l, bank(("o", h, t)), 0, t, h))
                after_drain(dve, l, ("o", 1, 1))
                norm_rows(l, 1, x_tok, 48 * l + 32, ln1_done)
                turn(l, "turn2", SHIFT2, SCALE2)

                def small(i):
                    return r_small[:, i]

                def groups(a):
                    return a.rearrange("p n (g e) -> p (n g) e", g=GROUPS)

                def over(ap, dim, shape):
                    return ap.unsqueeze(dim).broadcast_to(shape)

                LOG, EXP, SCORE, SEL, CHOSEN, CS, MASK, MS, G, PREF, DST, POS, W0 = range(13)
                filled(dve, l, ("logits", 0))
                drain(v.tensor_copy(small(LOG), bank(("logits", 0))[:, 0:TT * EXPERTS].rearrange("p (n e) -> p n e", n=TT)))
                after_drain(dve, l, ("logits", 0))
                red = r_small[:, W0]
                then(l, v.tensor_reduce(red[:, 0, 0:TT], small(LOG), AX_X, ALU.max))
                v.tensor_tensor(small(LOG), small(LOG), over(red[:, 0, 0:TT], 2, [P, TT, EXPERTS]), ALU.subtract).then_inc(max_ready, 1)
                dve.wait_ge(exp_ready, l + 1)
                then(l, v.tensor_reduce(red[:, 0, 2:2 + TT], small(EXP), AX_X, ALU.add))
                then(l, v.reciprocal(red[:, 0, 4:4 + TT], red[:, 0, 2:2 + TT]))
                then(l, v.tensor_tensor(small(SCORE), small(EXP), over(red[:, 0, 4:4 + TT], 2, [P, TT, EXPERTS]), ALU.mult))
                then(l, v.tensor_tensor(small(SEL), small(SCORE), brout_sb[:].unsqueeze(1).broadcast_to([P, TT, EXPERTS]), ALU.add))
                dve.wait_ge(moe_consts_in, 32 * (l + 1))

                def beaten(src, rows_n, out_ap, gt, eq):
                    four = [P, rows_n, PER_GROUP, PER_GROUP]
                    other, own = src.unsqueeze(2).broadcast_to(four), src.unsqueeze(3).broadcast_to(four)
                    tri = tri16[:, 0:PER_GROUP, 0:PER_GROUP]
                    n = rows_n * PER_GROUP * PER_GROUP
                    g4 = r_wide[:, gt, 0:n].rearrange("p (r a b) -> p r a b", r=rows_n, a=PER_GROUP)
                    e4 = r_wide[:, eq, 0:n].rearrange("p (r a b) -> p r a b", r=rows_n, a=PER_GROUP)
                    then(l, v.tensor_tensor(g4, other, own, ALU.is_gt))
                    then(l, v.tensor_tensor(e4, other, own, ALU.is_equal))
                    then(l, v.tensor_tensor(e4, e4, tri.unsqueeze(1).broadcast_to(four), ALU.mult))
                    then(l, v.tensor_tensor(g4, g4, e4, ALU.add))
                    then(l, v.tensor_reduce(out_ap, g4, AX_X, ALU.add))

                rank = r_small[:, W0 + 1]
                beaten(groups(small(SEL)), TT * GROUPS, groups(rank), 0, 1)
                then(l, v.tensor_scalar(small(CHOSEN), rank, TOP_K - 0.5, None, ALU.is_lt))
                then(l, v.tensor_tensor(small(CS), small(CHOSEN), small(SEL), ALU.mult))
                gscore = red[:, 1, 0:TT * GROUPS]
                then(l, v.tensor_reduce(gscore, groups(small(CS)), AX_X, ALU.add))
                grank = red[:, 1, TT * GROUPS:2 * TT * GROUPS]
                beaten(gscore.rearrange("p (n g) -> p n g", n=TT), TT, grank.rearrange("p (n g) -> p n g", n=TT), 0, 1)
                then(l, v.tensor_scalar(grank, grank, 0.5, None, ALU.is_lt))
                then(l, v.tensor_tensor(groups(small(MASK)), groups(small(CHOSEN)),
                                        grank.unsqueeze(2).broadcast_to([P, TT * GROUPS, PER_GROUP]), ALU.mult))
                v.tensor_tensor(small(MS), small(MASK), small(SCORE), ALU.mult).then_inc(mask_ready, 1)
                dve.wait_ge(mask_ready, l + 1)
                then(l, v.tensor_reduce(red[:, 0, 6:6 + TT], small(MS), AX_X, ALU.add))
                then(l, v.reciprocal(red[:, 0, 8:8 + TT], red[:, 0, 6:6 + TT]))
                then(l, v.tensor_tensor(small(G), small(MS), over(red[:, 0, 8:8 + TT], 2, [P, TT, EXPERTS]), ALU.mult))
                filled(dve, l, ("ranks", 0))
                rk = bank(("ranks", 0))
                count = r_small[:, W0 + 2, 0]
                v.tensor_copy(small(PREF), rk[:, 0:TT * EXPERTS].rearrange("p (n e) -> p n e", n=TT))
                drain(v.tensor_copy(count, rk[:, TT * EXPERTS:(TT + 1) * EXPERTS]))
                after_drain(dve, l, ("ranks", 0))
                start = r_small[:, W0 + 2, 1]
                s16 = r_wide[:, 2].rearrange("p (a b) -> p a b", a=EXPERTS)
                then(l, v.tensor_tensor(s16, tri16, count.unsqueeze(1).broadcast_to([P, EXPERTS, EXPERTS]), ALU.mult))
                then(l, v.tensor_reduce(start, s16, AX_X, ALU.add))
                then(l, v.tensor_tensor(small(DST), small(PREF), start.unsqueeze(1).broadcast_to([P, TT, EXPERTS]), ALU.add))
                lo, hi = small(W0 + 3), small(W0 + 4)
                then(l, v.tensor_scalar(lo, small(DST), -BIG, None, ALU.add))
                then(l, v.tensor_tensor(lo, lo, small(MASK), ALU.mult))
                then(l, v.tensor_reduce(red[:, 0, 10:10 + TT], lo, AX_X, ALU.min))
                then(l, v.tensor_scalar(red[:, 0, 10:10 + TT], red[:, 0, 10:10 + TT], BIG, None, ALU.add))
                then(l, v.tensor_scalar(hi, small(DST), 1.0, None, ALU.add))
                then(l, v.tensor_tensor(hi, hi, small(MASK), ALU.mult))
                then(l, v.tensor_reduce(red[:, 0, 12:12 + TT], hi, AX_X, ALU.max))
                then(l, v.tensor_scalar(red[:, 0, 12:12 + TT], red[:, 0, 12:12 + TT], -1.0, None, ALU.add))
                for t in range(TT):
                    then(l, v.tensor_scalar(onehot[:, t, :], iota, red[:, 0, 10 + t:11 + t], None, ALU.is_equal))
                    v.scalar_tensor_tensor(out=onehot[:, t, :], in0=iota, scalar=red[:, 0, 12 + t:13 + t], in1=onehot[:, t, :],
                                           op0=ALU.is_equal, op1=ALU.add).then_inc(onehot_ready, 1)
                nb = r_small[:, W0 + 5, 0]
                then(l, v.tensor_scalar(nb, count, float(BLOCK), 1.0, ALU.is_gt, ALU.add))
                for i in range(2, T // BLOCK):
                    then(l, v.scalar_tensor_tensor(out=nb, in0=count, scalar=float(i * BLOCK), in1=nb,
                                                   op0=ALU.is_gt, op1=ALU.add))
                v.tensor_copy(start_i[:], start[0:1, :])
                v.tensor_copy(blocks_i[:], nb[0:1, :]).then_inc(blocks_ready, 1)
                then(l, v.scalar_tensor_tensor(out=small(POS), in0=small(PREF), scalar=1.0, in1=small(MASK),
                                               op0=ALU.add, op1=ALU.mult))
                v.tensor_scalar(small(POS), small(POS), -1.0, None, ALU.add).then_inc(pos_step, 1)
                for k in range(1, KD, 2):
                    filled(dve, l, ("gather", k))
                    drain(v.tensor_scalar(sorted_ch[:, k, 0:SLOTS], bank(("gather", k))[:], mod[:, SCALE2, k:k + 1],
                                          mod[:, SHIFT2, k:k + 1], ALU.mult, ALU.add))
                after_drain(dve, l, ("gather", KD - 1))
                after_drain(dve, l, ("gather", KD - 2))
                dve.wait_ge(moe_zeroed, 4 * (l + 1))
                dve.wait_ge(blocks_ready, l + 1)
                alone(dve)

                def expert(pair, q):
                    e = 2 * pair + q
                    n = dve.value_load(blocks_i[0:1, bass.ds(e, 1)], min_val=1, max_val=T // BLOCK)
                    first = dve.value_load(start_i[0:1, bass.ds(e, 1)], min_val=0, max_val=SLOTS)
                    with dve.Fori(0, n) as i:
                        b = dve.snap(n_blk)
                        dve.wait_ge(h3_ready, b)
                        at_s = nc.s_assert_within(first + i * BLOCK, 0, SLOTS)
                        v.tensor_copy(xe, sorted_ch[:, :, bass.ds(at_s, BLOCK)]).then_inc(xe_ready, 1)
                        dve.wait_ge(turn_ready, b)
                        dve.wait_ge(pos_step, b + l)
                        for t in range(TT):
                            pos_c = small(POS)[:, t, bass.ds(e, 1)]
                            g_c = small(G)[:, t, bass.ds(e, 1)]
                            ins = v.tensor_scalar(pick[:, q, t, q * BLOCK:(q + 1) * BLOCK], iota[:, 0:BLOCK],
                                                  pos_c, g_c, ALU.is_equal, ALU.mult)
                        ins.then_inc(pick_ready, 1)
                        dve.wait_ge(pick_ready, b + 1)
                        col = small(POS)[:, :, bass.ds(e, 1)]
                        v.tensor_scalar(col, col, -float(BLOCK), None, ALU.add).then_inc(pos_step, 1)
                        dve.wait_ge(silu_ready, b + 1)
                        dve.wait_ge(h3_ready, b + 1)
                        v.tensor_tensor(hid, ps_h3[:, 0:T], silu_e, ALU.mult).then_inc(hid_ready, 1)
                        dve.reg_add(n_blk, n_blk, 1)

                with dve.Fori(0, MOE_PAIRS) as pair:
                    for q in range(2):
                        expert(pair, q)

                dve.wait_ge(moe_ready, l + 1)
                for h in range(2):
                    for t in range(TT):
                        ins = residual(l, moe_sum[t][h], 1, t, h)
                then(l, ins)
                norm_rows(l, 2, x_tok, 48 * l + 48, ln2_done)
                assert steps[0] == DVE_CHAIN, steps[0]

        @block.tensor
        def _(pe):
            mm = nc.tensor.matmul
            n_blk = pe.alloc_register("pe_block")
            pe.reg_mov(n_blk, PRIMED)
            pe.sem_inc(h1_ready, PRIMED)
            pe.sem_inc(h3_ready, PRIMED)
            pe.sem_inc(turn_ready, PRIMED)
            pe.sem_inc(y_ready, PRIMED)

            def open_bank(l, what):
                i = USE[what]
                if i >= BANKS:
                    after_drain(pe, l, USES[i - BANKS][0])
                return psum[i % BANKS]

            def fill(what, ins):
                ins.then_inc(bank_full, 1)

            def ada(n, ps):
                acc = ada_sum[:, n % 2, :]
                if ADA_PARTS[n] in (2, 5):
                    ins = mm(ps[:], ones[:], acc, start=True, stop=True)
                else:
                    for m in range(MT):
                        ins = mm(ps[:, m:m + 1], acc[:, m * P:(m + 1) * P], ones[:, 0:1], start=True, stop=True)
                ins.then_inc(bank_full, 1)

            def channel_major(l, unit, src):
                u = UNIT[unit]
                unit_loaded(pe, l, u)
                w = slot(u % RING)
                for i in range(2):
                    ps = open_bank(l, (*unit, i))
                    for j in range(2):
                        m = 2 * i + j
                        for k in range(KD):
                            ins = mm(ps[:, j * T:(j + 1) * T], w[:, k, m * P:(m + 1) * P], src[:, k, :],
                                     start=(k == 0), stop=(k == KD - 1))
                    fill((*unit, i), ins)

            def token_major(l, unit, src):
                u = UNIT[unit]
                unit_loaded(pe, l, u)
                w = slot(u % RING)
                for t in range(TT):
                    ps = open_bank(l, (*unit, t))
                    for k in range(KD):
                        ins = mm(ps[:], src[:, k, t * P:(t + 1) * P], w[:, k, :], start=(k == 0), stop=(k == KD - 1))
                    fill((*unit, t), ins)

            def turn(l, name):
                for i in range(KD // 2):
                    ps = open_bank(l, (name, i))
                    for j in range(2):
                        for t in range(TT):
                            ins = nc.tensor.transpose(ps[:, j * T + t * P:j * T + (t + 1) * P],
                                                      x_tok[:, t, (2 * i + j) * P:(2 * i + j + 1) * P], ident[:])
                    fill((name, i), ins)
                after_drain(pe, l, (name, KD // 2 - 2))
                after_drain(pe, l, (name, KD // 2 - 1))

            pe.wait_ge(consts_ready, 3)
            pe.wait_ge(params_in, 16 * 7)
            for n in range(NEXT):
                pe.wait_ge(ada_ready, n + 1)
                ada(n, psum[n])
            pe.wait_ge(drained["dve"], NEXT)
            with pe.Fori(0, DEPTH) as l:
                pe.wait_ge(ln2_done, l * TT + PRIMED)
                turn(l, "turn1")
                for what, n in PE_ORDER:
                    if what == "mix":
                        pe.wait_ge(sgv_ready, TT * (l + 1))
                        pe.wait_ge(sgw_masked, l + 1)
                        for i in range(HEADS // 2):
                            ps = open_bank(l, ("mix", i))
                            for j in range(2):
                                h = 2 * i + j
                                for t in range(TT):
                                    ins = mm(ps[:, j * T + t * P:j * T + (t + 1) * P], sg_v[:, t, h * P:(h + 1) * P],
                                             sg_wm[:, h, :], start=True, stop=True)
                            fill(("mix", i), ins)
                    elif what in ("mean", "var"):
                        ps = open_bank(l, (what, 0))
                        if what == "mean":
                            pe.wait_ge(conv_step, (l + 1) * KD * CV_TAPS)
                        else:
                            pe.wait_ge(cv_squared, l + 1)
                        for k in range(KD):
                            ins = mm(ps[:, 0:T], mean_w[:], (y_b if what == "mean" else cv_sq)[:, k, :],
                                     start=(k == 0), stop=(k == KD - 1))
                        fill((what, 0), ins)
                    elif what == "ada":
                        ps = open_bank(l, (what, n))
                        ada_summed(pe, l, n)
                        ada(n, ps)
                    elif what == "in":
                        (token_major if n >= 12 else channel_major)(l, (what, n), u_ch)
                    elif what == "gate":
                        channel_major(l, (what, n), u_ch)
                    elif what == "branch":
                        if n == (0, 0):
                            after_drain(pe, l, ("in", 1, 1))
                        if n == (1, 0):
                            pe.wait_ge(yb_ready, l + 1)
                        if n == (2, 0):
                            pe.wait_ge(yc_ready, (HEADS // 2) * (l + 1))
                        channel_major(l, (what, n), (y_a, y_b, y_c)[n[0]])
                    else:
                        if n == 0:
                            pe.wait_ge(merged_ready, 2 * (KD // MT) * (l + 1))
                        token_major(l, (what, n), merged)
                pe.wait_ge(ln1_done, TT * (l + 1))
                turn(l, "turn2")
                ps = open_bank(l, ("logits", 0))
                for t in range(TT):
                    for k in range(KD):
                        ins = mm(ps[:, t * EXPERTS:(t + 1) * EXPERTS], u_ch[:, k, t * P:(t + 1) * P], router_sb[:, k, :],
                                 start=(k == 0), stop=(k == KD - 1))
                fill(("logits", 0), ins)
                ps = open_bank(l, ("ranks", 0))
                mask = r_small[:, 6]
                pe.wait_ge(mask_ready, l + 1)
                mm(ps[:, 0:EXPERTS], prec[:], mask[:, 0], start=True, stop=True)
                mm(ps[:, EXPERTS:2 * EXPERTS], ones[:], mask[:, 0], start=True, stop=False)
                mm(ps[:, EXPERTS:2 * EXPERTS], prec[:], mask[:, 1], start=False, stop=True)
                mm(ps[:, 2 * EXPERTS:3 * EXPERTS], ones[:], mask[:, 0], start=True, stop=False)
                fill(("ranks", 0), mm(ps[:, 2 * EXPERTS:3 * EXPERTS], ones[:], mask[:, 1], start=False, stop=True))
                for k in range(KD):
                    ps = open_bank(l, ("gather", k))
                    pe.wait_ge(onehot_ready, TT * (l + 1))
                    for t in range(TT):
                        ins = mm(ps[:], x_tok[:, t, k * P:(k + 1) * P], onehot[:, t, :], start=(t == 0), stop=(t == TT - 1))
                    fill(("gather", k), ins)

                pe.wait_ge(blocks_ready, l + 1)
                pe.wait_ge(moe_zeroed, 4 * (l + 1))
                after_drain(pe, l, ("gather", KD - 1))
                after_drain(pe, l, ("gather", KD - 2))
                for t in range(TT):
                    for h in range(2):
                        mm(moe_sum[t][h][:], turned[:, 0:P], y_two[:, h * HALF:(h + 1) * HALF], start=True, stop=False, skip_group_check=True)

                def combine(last=False):
                    for t in range(TT):
                        for h in range(2):
                            ins = mm(moe_sum[t][h][:], turned[:, 2 * P + t * P:2 * P + (t + 1) * P],
                                     y_two[:, h * HALF:(h + 1) * HALF], start=False, stop=last, skip_group_check=True)
                    return ins

                def expert(l, pair, q):
                    s0 = 3 * q
                    e = 2 * pair + q
                    for i in range(3):
                        s = s0 + i
                        pe.wait_ge(unit_in[s], 16 * (l * PER_SLOT[s] + pair + (MIX[s] + 1 + (s < NEXT))))
                    n = pe.value_load(blocks_i[0:1, bass.ds(e, 1)], min_val=1, max_val=T // BLOCK)
                    with pe.Fori(0, n):
                        b = pe.snap(n_blk)
                        pe.wait_ge(xe_ready, b + 1)
                        for s, ps, ready in ((s0, ps_h1, h1_ready), (s0 + 1, ps_h3, h3_ready)):
                            w = slot(s)
                            for k in range(KD):
                                for h in range(2):
                                    ins = mm(ps[h * BLOCK:(h + 1) * BLOCK, 0:T], xe[:, k, :], w[:, k, h * T:(h + 1) * T],
                                             start=(k == 0), stop=(k == KD - 1))
                            ins.then_inc(ready, 1)
                        pe.wait_ge(y_copied, b)
                        combine()
                        pe.wait_ge(pick_ready, b + 1)
                        for t in range(TT):
                            nc.tensor.transpose(ps_turn[:, 2 * P + t * P:2 * P + (t + 1) * P],
                                                pick[:, q, t], ident[:])
                        pe.wait_ge(hid_ready, b + 1)
                        for c in range(2):
                            ins = nc.tensor.transpose(ps_turn[:, c * P:(c + 1) * P], hid[:, c * P:(c + 1) * P], ident[:])
                        ins.then_inc(turn_ready, 1)
                        pe.wait_ge(turned_ready, b + 1)
                        w = slot(s0 + 2, KE)
                        for f in range(KE):
                            half, c = f // 2, f % 2
                            for h in range(2):
                                ins = mm(ps_y[h * BLOCK:(h + 1) * BLOCK, :],
                                         turned[:, c * P + half * BLOCK:c * P + (half + 1) * BLOCK],
                                         w[:, f, h * HALF:(h + 1) * HALF], start=(f == 0), stop=(f == KE - 1))
                        ins.then_inc(y_ready, 1)
                        pe.reg_add(n_blk, n_blk, 1)

                with pe.Fori(0, MOE_PAIRS) as pair:
                    for q in range(2):
                        expert(l, pair, q)
                pe.wait_ge(y_copied, pe.snap(n_blk))
                combine(True).then_inc(moe_ready, 1)


def kernel(x, c, w_ada, b_ada, w_in, sc_conv, cv_conv, cv_conv_b, cv_ln_g, cv_ln_b, sg_ln_g, sg_ln_b,
           sg_w, sg_b, w_branch, w_gate, b_gate, w_o, ln1_g, ln1_b, w_router, b_router, w1, w3, w2,
           ln2_g, ln2_b):
    import numpy as np
    import concourse.bacc as bacc
    from concourse.bass_utils import run_bass_kernel_spmd

    def cols(a):
        return a.reshape(DEPTH, -1, KD, P).transpose(3, 0, 1, 2)

    ada = b_ada.reshape(DEPTH, 6, D)
    chan = np.concatenate([cols(ada[:, [0, 1, 3, 4]]), cols(sc_conv), cols(cv_conv), cols(cv_conv_b),
                           cols(cv_ln_g), cols(cv_ln_b), cols(b_gate)], axis=2)
    rows = np.stack([sg_ln_g, sg_ln_b, sg_b.reshape(DEPTH, D), ln1_g, ln1_b, ln2_g, ln2_b, ada[:, 2], ada[:, 5]], axis=1)
    i = np.arange(P)
    e = np.arange(EXPERTS)
    consts = np.zeros((P, N_CONST), np.float32)
    consts[:, C_ID:C_ID + P] = np.eye(P)
    consts[:, C_PREC:C_PREC + P] = i[:, None] < i[None, :]
    consts[:, C_TRI16:C_IOTA] = (e[None, :] < e[:, None]).reshape(1, -1)
    consts[:, C_IOTA:] = np.arange(SLOTS)[None, :]
    arrays = {
        "x": x.reshape(T, D), "c_cols": c.reshape(KD, P).T, "w_ada": w_ada, "w_in": w_in, "w_gate": w_gate,
        "w_branch": w_branch, "w_o": w_o, "w1": w1, "w3": w3, "w2": w2, "w_router": w_router,
        "b_router": b_router, "sg_wt": sg_w.transpose(0, 3, 1, 2), "chan": chan, "rows": rows, "consts": consts,
    }
    nc = bacc.Bacc("TRN2", target_bir_lowering=False, num_devices=1)
    feed, args = {}, []
    for name, a in arrays.items():
        a = np.ascontiguousarray(a)
        feed[f"in_{name}"] = a
        args.append(nc.dram_tensor(f"in_{name}", a.shape, mybir.dt.from_np(a.dtype), kind="ExternalInput").ap())
    args.append(nc.dram_tensor("out_x", (T, D), F32, kind="ExternalOutput").ap())
    build(nc, *args)
    result = run_bass_kernel_spmd(nc, [feed], core_ids=[0])
    return result.results[0]["out_x"].reshape(1, T, D)
```

```python
from contextlib import ExitStack

import concourse.bass as bass
from concourse import mybir

F32 = mybir.dt.float32
F32R = mybir.dt.float32r
I32 = mybir.dt.int32
ALU = mybir.AluOpType
ACT = mybir.ActivationFunctionType
AX_X = mybir.AxisListType.X

P = 128
DEPTH = 2
D = 1024
T = 256
TT = T // P
KD = D // P
HALF = D // 2
MT = HALF // P
SC_TAPS, CV_TAPS = 3, 31
HEADS = 8
EXPERTS, GROUPS = 16, 4
PER_GROUP = EXPERTS // GROUPS
TOP_K = 2
DE = 512
KE = DE // P
BLOCK = 64
SLOTS = TOP_K * T
ALPHA = (2.0 * DEPTH) ** 0.25
LN_EPS = 1e-5
PRIMED = 1
BIG = 4096.0

RING = 6
RAW = 4
CHUNKS = 4
KC = KD // CHUNKS
SLOT = KD * HALF
BANKS = 8
BANK = 512

SHIFT1, SCALE1, SHIFT2, SCALE2 = 0, 1, 2, 3
SC_W = 4
CV_W = SC_W + SC_TAPS
CV_B = CV_W + CV_TAPS
CV_G, CV_LB = CV_B + 1, CV_B + 2
B_GATE = CV_B + 3
LN1_G, LN1_B = B_GATE + 3, B_GATE + 4
N_CHAN = LN1_B + 1
ROW_SG, ROW_LN1, ROW_LN2, ROW_GATE = 0, 3, 5, 7
N_ROWS = 9
C_ID, C_PREC = 0, P
C_TRI16 = 2 * P
C_IOTA = C_TRI16 + EXPERTS * EXPERTS
C_FOLD = C_IOTA + SLOTS
QUAD = 32
N_CONST = C_FOLD + EXPERTS

ADA_PARTS = [0, 0, 1, 1, 2, 2, 3, 3, 4, 4, 5, 5]
NEXT = 4
UNITS = [("in", 8), ("in", 6), ("ada", 4), ("ada", 5), ("in", 9), ("in", 7),
         ("in", 12), ("in", 13), ("in", 2), ("in", 4), ("in", 3), ("in", 5),
         ("in", 10), ("in", 11), ("gate", (0, 0)), ("gate", (0, 1)), ("in", 0), ("in", 1),
         ("ada", 6), ("gate", (2, 0)), ("ada", 7), ("gate", (2, 1)),
         ("branch", (0, 0)), ("ada", 8), ("branch", (0, 1)), ("ada", 9), ("gate", (1, 0)), ("gate", (1, 1)), ("ada", 10),
         ("branch", (2, 0)), ("ada", 11), ("branch", (2, 1)), ("ada", 0), ("branch", (1, 0)),
         ("ada", 1), ("branch", (1, 1)), ("o", 0), ("ada", 2), ("o", 1), ("ada", 3)]
PRODUCTS = [u for u in UNITS if u[0] != "ada"]
PE_ORDER = [("in", 8), ("in", 6), ("in", 9), ("ada", 4), ("ada", 5), ("in", 7), ("in", 12), ("in", 13),
            ("in", 2), ("in", 4), ("in", 3), ("in", 5), ("in", 10), ("in", 11), ("gate", (0, 0)), ("gate", (0, 1)),
            ("in", 0), ("in", 1), ("mix", 0), ("mean", 0), ("gate", (2, 0)), ("ada", 6), ("ada", 7),
            ("gate", (2, 1)), ("var", 0), ("branch", (0, 0)), ("branch", (0, 1)),
            ("gate", (1, 0)), ("ada", 8), ("ada", 9), ("gate", (1, 1)), ("branch", (2, 0)), ("ada", 10), ("ada", 11),
            ("branch", (2, 1)), ("branch", (1, 0)), ("ada", 0), ("ada", 1), ("branch", (1, 1)),
            ("o", 0), ("ada", 2), ("o", 1), ("ada", 3)]
assert PRODUCTS == [u for u in PE_ORDER if u in PRODUCTS]
ADA_ORDER = [n for what, n in PE_ORDER if what == "ada"]
UNIT = {u: i for i, u in enumerate(UNITS)}
MIX = [len(range(s, len(UNITS), RAW)) if s < RAW else 0 for s in range(RING)]
MOE_PAIRS = EXPERTS // 2
PER_SLOT = [m + MOE_PAIRS for m in MIX]


def bank_uses():
    by_act = {8, 9, 12, 13, 2, 3, 10, 11}
    uses = [(("turn1", i), "act" if i % 2 == 0 else "dve") for i in range(KD // 2)]
    for what, n in PE_ORDER:
        if what == "mix":
            uses += [(("mix", i), "dve") for i in range(HEADS // 2)]
        elif what in ("mean", "ada"):
            uses.append(((what, n), "dve"))
        elif what == "var":
            uses.append(((what, n), "act"))
        else:
            who = "act" if what == "gate" or (what == "in" and n in by_act) else "dve"
            uses += [((what, n, i), who) for i in range(2)]
    uses += [(("turn2", i), "act" if i % 2 == 0 else "dve") for i in range(KD // 2)]
    uses += [(("partial", 0), "dve"), (("logits", 0), "dve"), (("ranks", 0), "dve")]
    uses += [(("gather", i), "act" if i % 2 == 0 else "dve") for i in range(KD)]
    return uses


USES = bank_uses()
USE = {what: i for i, (what, _) in enumerate(USES)}
N_USES = len(USES)
N_DRAINED = {e: sum(w == e for _, w in USES) for e in ("act", "dve")}
DRAINED = {what: (e, sum(w == e for _, w in USES[:i + 1])) for i, (what, e) in enumerate(USES)}
DVE_CHAIN = 178


def build(nc, x, c_cols, w_ada, w_in, w_gate, w_branch, w_o, w1, w3, w2, w_router, b_router,
          sg_wt, chan, rows, consts, out):
    ctx = ExitStack()
    with ctx:
        def sb(name, shape, dt=F32):
            return ctx.enter_context(nc.sbuf_tensor(name, shape, dt))

        def next_base():
            return -(-nc.sbuf_base // 32) * 32

        def split_part(name, base, shape):
            return nc.alloc_sbuf_tensor_at(name, shape, F32R, offset=base)

        def sem(name):
            return ctx.enter_context(nc.semaphore(name))

        ring_base = next_base()
        ring = sb("ring", [P, RING, SLOT])
        x_tok = sb("x_tok", [P, TT, D])
        u_base = next_base()
        u_ch = sb("u_ch", [P, KD, T])
        rows_base = next_base()
        row_buf = sb("row_buf", [P, 3, D])
        gate_row = sb("gate_row", [P, 2, D])
        chan_sb = sb("chan_sb", [P, DEPTH, N_CHAN, KD])
        mod = sb("mod", [P, 4, KD])
        fold = sb("fold", [P, KD])
        c_act = sb("c_act", [P, KD])
        ada_sum = sb("ada_sum", [P, 2, HALF])
        ones = sb("ones", [P, P])
        mean_w = sb("mean_w", [P, P])
        ident = sb("ident", [P, P])
        prec = sb("prec", [P, P])
        router_sb = sb("router_sb", [P, KD, QUAD])
        quad_sum = sb("quad_sum", [P, EXPERTS])
        brout_sb = sb("brout_sb", [P, EXPERTS])
        eps = sb("eps", [P, 1])
        stats = sb("stats", [P, TT, 2, 6])
        aggr = sb("aggr", [P, TT, 2])
        std = sb("std", [P, TT])
        rstd = sb("rstd", [P, TT])
        blocks_i = sb("blocks_i", [1, EXPERTS], I32)
        start_i = sb("start_i", [1, EXPERTS], I32)
        CV_PAD = CV_TAPS - 1
        SC_PAD = SC_TAPS - 1
        cv_in_n, sc_in_n, full = KD * (T + CV_PAD), KD * (T + SC_PAD), KD * T
        shared_n = 5 * full + cv_in_n + sc_in_n + 2 * BANK + HEADS * P
        shared_base = next_base()
        shared = sb("shared", [P, shared_n])
        at = [0]

        def part(n):
            at[0] += n
            return shared[:, at[0] - n:at[0]]

        gate_a = part(full).rearrange("p (k t) -> p k t", k=KD)
        sc_part = part(sc_in_n)
        sc_in = sc_part.rearrange("p (k t) -> p k t", k=KD)
        gate_b = sc_part[:, 0:full].rearrange("p (k t) -> p k t", k=KD)
        ya_base = shared_base + 4 * at[0]
        y_a = part(full).rearrange("p (k t) -> p k t", k=KD)
        cv_base = shared_base + 4 * at[0]
        cv_part = part(cv_in_n)
        cv_in = cv_part.rearrange("p (k t) -> p k t", k=KD)
        yb_base = shared_base + 4 * at[0]
        y_b = part(full).rearrange("p (k t) -> p k t", k=KD)
        yc_at = at[0]
        yc_base = shared_base + 4 * yc_at
        y_c = part(full).rearrange("p (k t) -> p k t", k=KD)
        sg_base = shared_base + 4 * at[0]
        sg_flat = part(full)
        sg_v = sg_flat.rearrange("p (n c) -> p n c", n=TT)
        merged = sg_flat.rearrange("p (k t) -> p k t", k=KD)
        tmp = part(2 * BANK).rearrange("p (b n) -> p b n", b=2)
        wm_part = part(HEADS * P)
        sg_wm = wm_part.rearrange("p (h t) -> p h t", h=HEADS)
        sg_rows = sc_part[:, 0:2 * D].rearrange("p (v d) -> p v d", v=2)
        glu_sig = gate_a
        cv_sq = merged
        cv_std, cv_rstd = wm_part[:, 0:T], wm_part[:, T:2 * T]
        w_lo = split_part("w_lo", ring_base, [P, RAW, KD, HALF])
        w_hi = split_part("w_hi", ring_base + 4 * RAW * SLOT, [P, RING - RAW, KD, HALF])
        u_lo = split_part("u_lo", u_base, [P, KD, T])
        u_hi = split_part("u_hi", rows_base, [P, KD, T])
        ya_lo, yb_lo, yc_lo, merged_lo = (split_part(n, b, [P, KD, T]) for n, b in (
            ("ya_lo", ya_base), ("yb_lo", yb_base), ("yc_lo", yc_base), ("merged_lo", sg_base)))
        cv_hi = split_part("cv_hi", cv_base, [P, KD, T])
        yb_hi = split_part("yb_hi", ya_base, [P, KD, T])

        at[0] = 0
        SORTED = SLOTS + BLOCK
        sorted_ch = part(KD * SORTED).rearrange("p (k s) -> p k s", k=KD)
        onehot = split_part("onehot", shared_base + 4 * at[0], [P, TT, SLOTS])
        at[0] += TT * SLOTS
        xe = part(KD * BLOCK).rearrange("p (k s) -> p k s", k=KD)
        silu_e = part(T)
        hid = part(T)
        turned = part(BANK)
        y_two = part(D)
        pick = part(TT * P).rearrange("p (n s) -> p n s", n=TT)
        r_small = part(24 * TT * EXPERTS).rearrange("p (v n e) -> p v n e", v=24, n=TT)
        r_wide = part(3 * EXPERTS * EXPERTS).rearrange("p (v n) -> p v n", v=3)
        assert at[0] <= yc_at
        at[0] = yc_at
        iota = part(SLOTS)
        tri16 = part(EXPERTS * EXPERTS).rearrange("p (a b) -> p a b", a=EXPERTS)
        x_hi, x_lo = (split_part(n, shared_base + 4 * (at[0] + i * TT * D), [P, TT, D]) for i, n in enumerate(("x_hi", "x_lo")))
        at[0] += 2 * TT * D
        assert at[0] <= shared_n

        psum = [ctx.enter_context(nc.psum_tensor(f"bank{b}", [P, BANK], F32)) for b in range(BANKS)]
        moe_sum = [[psum[2 * n + h] for h in range(2)] for n in range(TT)]
        ps_h1, ps_h3, ps_turn, ps_y = psum[4], psum[5], psum[6], psum[7]

        c_in, chan_in = sem("c_in"), sem("chan_in")
        params_in = sem("params_in")
        consts_ready = sem("consts_ready")
        c_ready = sem("c_ready")
        unit_in = [sem(f"unit_in{s}") for s in range(RING)]
        bank_full = sem("bank_full")
        drained = {"act": sem("act_drained"), "dve": sem("dve_drained")}
        chain = sem("chain")
        first_chain = sem("first_chain")
        ada_ready = sem("ada_ready")
        w_hi_ready, w_lo_ready, w_read = sem("w_hi_ready"), sem("w_lo_ready"), sem("w_read")
        u_hi_ready, u_lo_ready = sem("u_hi_ready"), sem("u_lo_ready")
        y_hi_ready, y_lo_ready = sem("y_hi_ready"), sem("y_lo_ready")
        conv_step = sem("conv_step")
        rows_in, gates_in, sgw_in, moe_consts_in = sem("rows_in"), sem("gates_in"), sem("sgw_in"), sem("moe_consts_in")
        pads_ready = sem("pads_ready")
        sgw_masked = sem("sgw_masked")
        sgv_ready = sem("sgv_ready")
        ln_var, ln_std = sem("ln_var"), sem("ln_std")
        ln1_done = sem("ln1_done")
        yc_ready = sem("yc_ready")
        cv_squared, cv_normed, yb_ready = (
            sem("cv_squared"), sem("cv_normed"), sem("yb_ready"))
        merged_ready = sem("merged_ready")
        x_step = sem("x_step")
        x_hi_ready, x_lo_ready = sem("x_hi_ready"), sem("x_lo_ready")
        max_ready, exp_ready = sem("max_ready"), sem("exp_ready")
        mask_ready, onehot_ready, blocks_ready = sem("mask_ready"), sem("onehot_ready"), sem("blocks_ready")
        moe_zeroed, pos_step = sem("moe_zeroed"), sem("pos_step")
        xe_ready, pick_ready = sem("xe_ready"), sem("pick_ready")
        h1_ready, h3_ready, silu_ready, hid_ready = sem("h1_ready"), sem("h3_ready"), sem("silu_ready"), sem("hid_ready")
        turn_ready, turned_ready, y_ready, y_copied = sem("turn_ready"), sem("turned_ready"), sem("y_ready"), sem("y_copied")
        moe_ready, ln2_done, out_done = sem("moe_ready"), sem("ln2_done"), sem("out_done")

        passed = {e: sem(f"passed_{e}") for e in ("SP", "Pool", "DVE", "Activation")}

        ada_v = w_ada.rearrange("l (k p) n -> l p k n", p=P)
        in_v = w_in.rearrange("l (k p) n -> l p k n", p=P)
        gate_v = w_gate.rearrange("l (k p) b n -> l p k b n", p=P)
        branch_v = w_branch.rearrange("l b (k p) n -> l b p k n", p=P)
        o_v = w_o.rearrange("l (k p) n -> l p k n", p=P)
        w1_v = w1.rearrange("l e (k p) f -> l e p k f", p=P)
        w3_v = w3.rearrange("l e (k p) f -> l e p k f", p=P)
        w2_v = w2.rearrange("l e (k p) n -> l e p k n", p=P)

        def slot(s, k=KD):
            return ring[:, s, :].rearrange("p (k n) -> p k n", k=k)

        def unit_dram(u, l):
            what, n = UNITS[u]
            cols = lambda i: slice(i * HALF, (i + 1) * HALF)
            if what == "ada":
                if n < NEXT:
                    return ada_v[(l + 1) % DEPTH][:, :, cols(n)]
                return ada_v[l][:, :, cols(n)]
            if what == "in":
                return in_v[l][:, :, cols(n)]
            if what == "gate":
                return gate_v[l][:, :, n[0], cols(n[1])]
            if what == "branch":
                return branch_v[l, n[0]][:, :, cols(n[1])]
            return o_v[l][:, :, cols(n)]

        def alone(eng):
            eng.sem_inc(passed[eng.engine.name], 1)

        def unit_loaded(eng, l, u):
            eng.wait_ge(unit_in[u % RAW], 16 * (l * PER_SLOT[u % RAW] + (u // RAW + 2)))

        def chunk(c):
            return slice(c * KC, (c + 1) * KC)

        def w_raw(u):
            return slot(u % RAW)

        def ada_summed(eng, l, n):
            eng.wait_ge(ada_ready, len(ADA_PARTS) * l + (NEXT + ADA_ORDER.index(n) + 1))

        def unit_read(eng, l, u):
            what, n = UNITS[u]
            if what == "ada":
                ada_summed(eng, l, n)
            else:
                filled(eng, l, (what, n, 1))

        def filled(eng, l, what):
            eng.wait_ge(bank_full, l * N_USES + (NEXT + USE[what] + 1))

        def after_drain(eng, l, what):
            who, n = DRAINED[what]
            eng.wait_ge(drained[who], l * N_DRAINED[who] + (n + (NEXT if who == "dve" else 0)))

        def bank(what):
            return psum[USE[what] % BANKS]

        block = ctx.enter_context(nc.Block())

        @block.sync
        def _(sp):
            sp.dma_start(c_act[:], c_cols).then_inc(c_in, 16)

            def first_ada(n):
                sp.dma_start(slot(n), ada_v[0][:, :, n * HALF:(n + 1) * HALF]).then_inc(unit_in[n], 16)

            first_ada(0)
            first_ada(1)
            sp.dma_start(chan_sb[:], chan).then_inc(chan_in, 16)
            first_ada(2)
            first_ada(3)
            sp.dma_start(x_tok[:], x.rearrange("(n p) d -> p n d", p=P)).then_inc(params_in, 16)
            sp.dma_start(ident[:], consts[:, C_ID:C_ID + P]).then_inc(params_in, 16)
            sp.dma_start(prec[:], consts[:, C_PREC:C_PREC + P]).then_inc(params_in, 16)
            sp.dma_start(quad_sum[:], consts[:, C_FOLD:C_FOLD + EXPERTS]).then_inc(params_in, 16)
            sp.wait_ge(consts_ready, 4)
            sp.dma_start(router_sb[:, :, 0:EXPERTS], w_router.rearrange("(k p) e -> p k e", p=P)).then_inc(params_in, 16)
            sp.dma_start(brout_sb[:], b_router.partition_broadcast(P)).then_inc(params_in, 16)
            done = sp.alloc_register("blocks_done")
            sp.reg_mov(done, PRIMED)
            with sp.Fori(0, DEPTH) as l:
                for u in range(len(UNITS)):
                    if u < NEXT:
                        sp.wait_ge(ada_ready, len(ADA_PARTS) * l + u + 1)
                        alone(sp)
                    if u < RAW:
                        sp.wait_ge(y_ready, sp.snap(done))
                    else:
                        unit_read(sp, l, u - RAW)
                    alone(sp)
                    sp.dma_start(w_raw(u), unit_dram(u, l)).then_inc(unit_in[u % RAW], 16)

                def mixer_left(s, _):
                    if s < RAW:
                        unit_read(sp, l, max(range(s, len(UNITS), RAW)))
                    else:
                        unit_read(sp, l, UNIT[PRODUCTS[s - RING]])

                def expert(e, s0, wait):
                    for i, (src, k) in enumerate(((w1_v, KD), (w3_v, KD), (w2_v, KE))):
                        wait(s0 + i, (h1_ready, h3_ready, y_ready)[i])
                        alone(sp)
                        sp.dma_start(slot(s0 + i, k), src[l, e]).then_inc(unit_in[s0 + i], 16)

                for e in range(2):
                    expert(e, 3 * e, mixer_left)
                sp.wait_ge(blocks_ready, l + 1)
                alone(sp)
                with sp.Fori(1, MOE_PAIRS) as pair:
                    for q in range(2):
                        n = sp.value_load(blocks_i[0:1, bass.ds(2 * pair + (q - 2), 1)], min_val=1, max_val=T // BLOCK)
                        sp.reg_add(done, done, n)
                        expert(2 * pair + q, 3 * q, lambda _, last_read: sp.wait_ge(last_read, sp.snap(done)))
                for e in (EXPERTS - 2, EXPERTS - 1):
                    n = sp.value_load(blocks_i[0:1, e:e + 1], min_val=1, max_val=T // BLOCK)
                    sp.reg_add(done, done, n)
            for t in range(TT):
                sp.wait_ge(ln2_done, (DEPTH - 1) * TT + (t + 1 + PRIMED))
                sp.dma_start(out[t * P:(t + 1) * P], x_tok[:, t, :]).then_inc(out_done, 16)
            sp.wait_ge(out_done, 16 * TT)

        @block.gpsimd
        def _(pool):
            nc.gpsimd.memset(ones[:], 1.0).then_inc(consts_ready, 1)
            nc.gpsimd.memset(mean_w[:], 1.0 / D).then_inc(consts_ready, 1)
            nc.gpsimd.memset(eps[:], LN_EPS).then_inc(consts_ready, 1)
            nc.gpsimd.memset(router_sb[:], 0.0).then_inc(consts_ready, 1)
            with pool.Fori(0, DEPTH) as l:
                pool.wait_ge(ln2_done, l * TT + PRIMED)
                pool.wait_ge(ada_ready, len(ADA_PARTS) * l + NEXT)
                alone(pool)
                pool.dma_start(sg_rows, rows[l, ROW_SG:ROW_SG + 2].partition_broadcast(P)).then_inc(rows_in, 16)
                pool.dma_start(row_buf[:, 2, :], rows[l, ROW_SG + 2].partition_broadcast(P)).then_inc(rows_in, 16)
                pool.dma_start(gate_row[:, :, :], rows[l, ROW_GATE:ROW_GATE + 2].partition_broadcast(P)).then_inc(gates_in, 16)
                pool.dma_start(sg_wm, sg_wt[l]).then_inc(sgw_in, 16)
                nc.gpsimd.memset(cv_in[:, :, 0:CV_PAD], 0.0).then_inc(pads_ready, 1)
                for m, unit in enumerate(PRODUCTS):
                    u = UNIT[unit]
                    unit_loaded(pool, l, u)
                    alone(pool)
                    for c in range(CHUNKS):
                        pool.wait_ge(w_hi_ready, l * (len(PRODUCTS) * CHUNKS) + (m * CHUNKS + c + 1))
                        nc.gpsimd.tensor_tensor(w_lo[:, u % RAW, chunk(c), :], w_raw(u)[:, chunk(c), :],
                                                w_hi[:, m % 2, chunk(c), :], ALU.subtract).then_inc(w_lo_ready, 1)
                    if m == 2:
                        pool.wait_ge(sgw_in, 16 * (l + 1))
                        alone(pool)
                        nc.gpsimd.affine_select(out=sg_wm, in_=sg_wm, compare_op=ALU.is_ge, fill=0.0, base=0,
                                                pattern=[[0, HEADS], [1, P]], channel_multiplier=-1).then_inc(sgw_masked, 1)
                    if unit == ("branch", (2, 1)):
                        filled(pool, l, ("gate", (1, 1), 1))
                        pool.dma_start(row_buf[:, 0:2, :], rows[l, ROW_LN1:ROW_LN1 + 2].partition_broadcast(P)).then_inc(rows_in, 16)
                    if unit == ("o", 0):
                        filled(pool, l, ("branch", (2, 1), 1))
                        alone(pool)
                        pool.dma_start(iota, consts[:, C_IOTA:C_IOTA + SLOTS]).then_inc(moe_consts_in, 16)
                        pool.dma_start(tri16, consts[:, C_TRI16:C_IOTA].rearrange("p (a b) -> p a b", a=EXPERTS)).then_inc(moe_consts_in, 16)
                for t in range(TT):
                    pool.wait_ge(x_hi_ready, TT * l + t + 1)
                    nc.gpsimd.tensor_tensor(x_lo[:, t, :], x_tok[:, t, :], x_hi[:, t, :], ALU.subtract).then_inc(x_lo_ready, 1)
                nc.gpsimd.memset(sorted_ch[:, :, SLOTS:SORTED], 0.0).then_inc(moe_zeroed, 1)
                nc.gpsimd.memset(y_two, 0.0).then_inc(moe_zeroed, 1)
                nc.gpsimd.memset(turned, 0.0).then_inc(moe_zeroed, 1)
                nc.gpsimd.memset(pick, 0.0).then_inc(moe_zeroed, 1)
                filled(pool, l, ("turn2", KD // 2 - 1))
                pool.wait_ge(rows_in, 64 * l + 48)
                alone(pool)
                for v in range(2):
                    for t in range(TT):
                        if v:
                            pool.wait_ge(x_step, 2 * TT * l + t + 1)
                        nc.gpsimd.tensor_tensor(x_tok[:, t, :], x_tok[:, t, :], row_buf[:, v, :],
                                                (ALU.mult, ALU.add)[v]).then_inc(x_step, 1)
                pool.wait_ge(x_step, 2 * TT * (l + 1))
                alone(pool)
                pool.dma_start(row_buf[:, 0:2, :], rows[l, ROW_LN2:ROW_LN2 + 2].partition_broadcast(P)).then_inc(rows_in, 16)

        @block.scalar
        def _(act):
            act.wait_ge(c_in, 16)
            nc.scalar.activation(c_act[:], c_act[:], ACT.Silu).then_inc(c_ready, 1)
            act.wait_ge(consts_ready, 4)
            n_blk = act.alloc_register("act_block")
            act.reg_mov(n_blk, PRIMED)
            act.sem_inc(silu_ready, PRIMED)
            act.sem_inc(turned_ready, PRIMED)
            act.sem_inc(y_copied, PRIMED)
            act.wait_ge(chan_in, 16)

            def turn(l, name, which, shift, scale):
                for i in range(0, KD // 2, 2):
                    filled(act, l, (name, i))
                    for j in range(2):
                        k = 2 * i + j
                        ins = nc.scalar.activation(u_ch[:, k, :], bank((name, i))[:, j * T:(j + 1) * T], ACT.Identity,
                                                   bias=mod[:, shift, k:k + 1], scale=mod[:, scale, k:k + 1])
                    ins.then_inc(drained["act"], 1)

            def pairs(l, unit, dst, func):
                for i in range(2):
                    filled(act, l, (*unit, i))
                    nc.scalar.activation(dst(i), bank((*unit, i))[:], func).then_inc(drained["act"], 1)

            def two(buf, col, i):
                k = MT * col + 2 * i
                return buf[:, k:k + 2, :].rearrange("p k t -> p (k t)")

            def gates(l, b, dst, col):
                for i in range(2):
                    filled(act, l, ("gate", (b, col), i))
                    for j in range(2):
                        k = MT * col + 2 * i + j
                        ins = nc.scalar.activation(dst[:, k, :], bank(("gate", (b, col), i))[:, j * T:(j + 1) * T],
                                                   ACT.Sigmoid, bias=chan_at(l, B_GATE + b, k))
                    ins.then_inc(drained["act"], 1)

            def chan_at(l, v, k):
                return chan_sb[:, bass.ds(l, 1), v, k:k + 1].rearrange("p a b -> p (a b)")

            def deviation(l, n):
                act.wait_ge(ln_var, 3 * l + n + 1)
                nc.scalar.activation(std[:], aggr[:, :, 1], ACT.Sqrt, bias=eps[:, 0:1]).then_inc(ln_std, 1)

            def split_unit(l, m):
                if m >= len(PRODUCTS):
                    return
                u = UNIT[PRODUCTS[m]]
                unit_loaded(act, l, u)
                alone(act)
                for c in range(CHUNKS):
                    if m >= 2:
                        if c < CHUNKS - 1:
                            act.wait_ge(w_read, l * (len(PRODUCTS) * (CHUNKS - 1)) + ((m - 2) * (CHUNKS - 1) + c + 1))
                        else:
                            filled(act, l, (*PRODUCTS[m - 2], 1))
                    nc.scalar.activation(w_hi[:, m % 2, chunk(c), :], w_raw(u)[:, chunk(c), :], ACT.Copy).then_inc(w_hi_ready, 1)

            def ahead(l, unit):
                split_unit(l, PRODUCTS.index(unit) + 2)

            with act.Fori(0, DEPTH) as l:
                split_unit(l, 0)
                turn(l, "turn1", 0, SHIFT1, SCALE1)
                for h in range(2):
                    after_drain(act, l, ("turn1", 2 * h))
                    after_drain(act, l, ("turn1", 2 * h + 1))
                    k = slice(h * MT, (h + 1) * MT)
                    nc.scalar.activation(u_hi[:, k, :], u_ch[:, k, :], ACT.Copy).then_inc(u_hi_ready, 1)
                split_unit(l, 1)
                for col in range(2):
                    ahead(l, ("in", 8 + col))
                    pairs(l, ("in", 8 + col), lambda i: two(glu_sig, col, i), ACT.Sigmoid)
                    ahead(l, ("in", 6 + col))
                for h in range(2):
                    ahead(l, ("in", 12 + h))
                    pairs(l, ("in", 12 + h), lambda i: sg_v[:, i, h * HALF:(h + 1) * HALF], ACT.Gelu_apprx_tanh)
                ahead(l, ("in", 2))
                pairs(l, ("in", 2), lambda i: two(y_a, 0, i), ACT.Copy)
                ahead(l, ("in", 4))
                deviation(l, 0)
                ahead(l, ("in", 3))
                pairs(l, ("in", 3), lambda i: two(y_a, 1, i), ACT.Copy)
                ahead(l, ("in", 5))
                for col in range(2):
                    ahead(l, ("in", 10 + col))
                    pairs(l, ("in", 10 + col), lambda i: two(y_c, col, i), ACT.Gelu_apprx_tanh)
                for col in range(2):
                    ahead(l, ("gate", (0, col)))
                    gates(l, 0, gate_a, col)
                ahead(l, ("in", 0))
                ahead(l, ("in", 1))
                after_drain(act, l, ("in", 1, 1))
                alone(act)
                nc.scalar.activation(cv_hi[:], y_a, ACT.Copy).then_inc(y_hi_ready, 1)
                after_drain(act, l, ("mean", 0))
                filled(act, l, ("mix", HEADS // 2 - 1))
                alone(act)
                nc.scalar.activation(cv_sq, y_b, ACT.Square).then_inc(cv_squared, 1)
                for col in range(2):
                    ahead(l, ("gate", (2, col)))
                    gates(l, 2, gate_b, col)
                filled(act, l, ("var", 0))
                nc.scalar.activation(cv_std, bank(("var", 0))[:, 0:T], ACT.Sqrt, bias=eps[:, 0:1]).then_inc(drained["act"], 1)
                ahead(l, ("branch", (0, 0)))
                act.wait_ge(cv_normed, l + 1)
                for k in range(KD):
                    ins = nc.scalar.activation(y_b[:, k, :], y_b[:, k, :], ACT.Silu, bias=chan_at(l, CV_LB, k),
                                               scale=chan_at(l, CV_G, k))
                ins.then_inc(yb_ready, 1)
                ahead(l, ("branch", (0, 1)))
                filled(act, l, ("branch", (0, 1), 1))
                act.wait_ge(yc_ready, (HEADS // 2) * (l + 1))
                alone(act)
                nc.scalar.activation(cv_hi[:], y_c, ACT.Copy).then_inc(y_hi_ready, 1)
                act.wait_ge(yb_ready, l + 1)
                nc.scalar.activation(yb_hi[:], y_b, ACT.Copy).then_inc(y_hi_ready, 1)
                after_drain(act, l, ("branch", (0, 1), 1))
                alone(act)
                for col in range(2):
                    ahead(l, ("gate", (1, col)))
                    gates(l, 1, gate_a, col)
                ahead(l, ("branch", (2, 0)))
                ahead(l, ("branch", (2, 1)))
                filled(act, l, ("branch", (2, 1), 1))
                for col in range(2):
                    ahead(l, ("branch", (1, col)))
                    act.wait_ge(merged_ready, 2 * (KD // MT) * l + 2 * (col + 1))
                    k = slice(col * MT, (col + 1) * MT)
                    nc.scalar.activation(cv_hi[:, k, :], merged[:, k, :], ACT.Copy).then_inc(y_hi_ready, 1)
                deviation(l, 1)
                turn(l, "turn2", 0, SHIFT2, SCALE2)
                for t in range(TT):
                    act.wait_ge(ln1_done, TT * l + t + 1)
                    nc.scalar.activation(x_hi[:, t, :], x_tok[:, t, :], ACT.Copy).then_inc(x_hi_ready, 1)
                act.wait_ge(max_ready, l + 1)
                nc.scalar.activation(r_small[:, 1], r_small[:, 0], ACT.Exp).then_inc(exp_ready, 1)
                for k in range(0, KD, 2):
                    filled(act, l, ("gather", k))
                    nc.scalar.activation(sorted_ch[:, k, 0:SLOTS], bank(("gather", k))[:], ACT.Identity,
                                         bias=mod[:, SHIFT2, k:k + 1],
                                         scale=mod[:, SCALE2, k:k + 1]).then_inc(drained["act"], 1)
                act.wait_ge(blocks_ready, l + 1)
                act.wait_ge(moe_zeroed, 4 * (l + 1))

                def expert(pair, q):
                    e = 2 * pair + q
                    n = act.value_load(blocks_i[0:1, bass.ds(e, 1)], min_val=1, max_val=T // BLOCK)
                    with act.Fori(0, n):
                        b = act.snap(n_blk)
                        act.wait_ge(h1_ready, b + 1)
                        nc.scalar.activation(silu_e, ps_h1[:, 0:T], ACT.Silu).then_inc(silu_ready, 1)
                        act.wait_ge(turn_ready, b + 1)
                        nc.scalar.activation(turned[:, 0:2 * P], ps_turn[:, 0:2 * P], ACT.Copy).then_inc(turned_ready, 1)
                        nc.scalar.activation(turned[:, 2 * P:4 * P], ps_turn[:, 2 * P:4 * P], ACT.Copy)
                        act.wait_ge(y_ready, b + 1)
                        for h in range(2):
                            ins = nc.scalar.activation(y_two[q * BLOCK:(q + 1) * BLOCK, h * HALF:(h + 1) * HALF],
                                                       ps_y[h * BLOCK:(h + 1) * BLOCK, :], ACT.Copy)
                        ins.then_inc(y_copied, 1)
                        act.reg_add(n_blk, n_blk, 1)

                with act.Fori(0, MOE_PAIRS) as pair:
                    for q in range(2):
                        expert(pair, q)
                deviation(l, 2)

        @block.vector
        def _(dve):
            v = nc.vector
            steps = [0]
            n_blk = dve.alloc_register("dve_block")
            dve.reg_mov(n_blk, PRIMED)
            dve.sem_inc(xe_ready, PRIMED)
            dve.sem_inc(pick_ready, PRIMED)
            dve.sem_inc(hid_ready, PRIMED)
            dve.sem_inc(ln2_done, PRIMED)

            def chan_at(l, n, k):
                return chan_sb[:, bass.ds(l, 1), n, k:k + 1].rearrange("p a b -> p (a b)")

            def chan_all(l, n):
                return chan_sb[:, bass.ds(l, 1), n, :].rearrange("p a b -> p (a b)")

            def then(l, ins):
                steps[0] += 1
                ins.then_inc(chain, 1)
                dve.wait_ge(chain, l * DVE_CHAIN + steps[0])

            def drain(ins):
                ins.then_inc(drained["dve"], 1)

            first_steps = [0]

            def link_first(ins):
                first_steps[0] += 1
                ins.then_inc(first_chain, 1)
                dve.wait_ge(first_chain, first_steps[0])

            def ada_sums(l, n, w, before, link):
                acc = ada_sum[:, n % 2, :]
                before()
                link(v.tensor_scalar(acc, w[:, 0, :], c_act[:, 0:1], None, ALU.mult))
                for k in range(1, KD):
                    ins = v.scalar_tensor_tensor(out=acc, in0=w[:, k, :], scalar=c_act[:, k:k + 1], in1=acc,
                                                 op0=ALU.mult, op1=ALU.add)
                    if k < KD - 1:
                        link(ins)
                ins.then_inc(ada_ready, 1)

            def ada_unit(l, n):
                u = UNIT[("ada", n)]
                unit_loaded(dve, l, u)
                i = ADA_ORDER.index(n)
                ada_sums(l, n, w_raw(u), lambda: filled(dve, l, ("ada", ADA_ORDER[i - 2])) if i >= 2 else None,
                         lambda ins: then(l, ins))

            def ada_store(l, n, ps):
                part, half = ADA_PARTS[n], n % 2
                if part in (2, 5):
                    row = gate_row[:, part // 5, half * HALF:(half + 1) * HALF]
                    return v.tensor_tensor(row, ps[:], row, ALU.add)
                m = {0: SHIFT1, 1: SCALE1, 3: SHIFT2, 4: SCALE2}[part]
                b = chan_sb[:, bass.ds(l, 1), m, half * MT:(half + 1) * MT].rearrange("p a b -> p (a b)")
                return v.scalar_tensor_tensor(out=mod[:, m, half * MT:(half + 1) * MT], in0=ps[:, 0:MT],
                                              scalar=1.0 if part in (1, 4) else 0.0, in1=b,
                                              op0=ALU.add, op1=ALU.add)

            def ada_out(l, n):
                filled(dve, l, ("ada", n))
                if ADA_PARTS[n] in (2, 5):
                    dve.wait_ge(gates_in, 16 * (l + 1))
                drain(ada_store((l + 1) % DEPTH if n < NEXT else l, n, bank(("ada", n))))

            def turn(l, name, shift, scale):
                for i in range(1, KD // 2, 2):
                    filled(dve, l, (name, i))
                    for j in range(2):
                        k = 2 * i + j
                        ins = v.tensor_scalar(u_ch[:, k, :], bank((name, i))[:, j * T:(j + 1) * T],
                                              mod[:, scale, k:k + 1], mod[:, shift, k:k + 1], ALU.mult, ALU.add)
                    drain(ins)

            def conv31(l, pair, nth):
                tiles = (2 * pair, 2 * pair + 1)
                base = l * (KD * CV_TAPS) + 2 * nth * CV_TAPS

                def step(j, a, at):
                    k = tiles[a]
                    if isinstance(j, int) and j == 0:
                        return v.tensor_scalar(y_b[:, k, :], cv_in[:, k, 0:T], chan_at(l, CV_W, k),
                                               chan_at(l, CV_B, k), ALU.mult, ALU.add).then_inc(conv_step, 1)
                    w = chan_sb[:, bass.ds(l, 1), bass.ds(j + CV_W, 1), k:k + 1].rearrange("p a b c -> p (a b c)")
                    dve.wait_ge(conv_step, at)
                    return v.scalar_tensor_tensor(out=y_b[:, k, :], in0=cv_in[:, k, bass.ds(j, T)], scalar=w,
                                                  in1=y_b[:, k, :], op0=ALU.mult, op1=ALU.add).then_inc(conv_step, 1)

                for a in range(2):
                    step(0, a, 0)
                unroll = 5
                with dve.Fori(0, (CV_TAPS - 1) // unroll) as r:
                    for i in range(unroll):
                        for a in range(2):
                            step(r * unroll + (i + 1), a, base + 2 * unroll * r + (2 * i + a + 1))

            def conv3(l, pair):
                for a in range(2):
                    k = 2 * pair + a
                    v.tensor_scalar(y_a[:, k, :], sc_in[:, k, 0:T], chan_at(l, SC_W, k), None,
                                    ALU.mult).then_inc(chain, 1)
                steps[0] += 2
                dve.wait_ge(chain, l * DVE_CHAIN + steps[0])
                for j in range(1, SC_TAPS):
                    for a in range(2):
                        k = 2 * pair + a
                        v.scalar_tensor_tensor(out=y_a[:, k, :], in0=sc_in[:, k, j:j + T],
                                               scalar=chan_at(l, SC_W + j, k), in1=y_a[:, k, :],
                                               op0=ALU.mult, op1=ALU.add).then_inc(chain, 1)
                    steps[0] += 2
                    dve.wait_ge(chain, l * DVE_CHAIN + steps[0])

            def flat(buf, col, i):
                k = MT * col + 2 * i
                return buf[:, k:k + 2, :]

            def ps2(what):
                return bank(what)[:].rearrange("p (k t) -> p k t", k=2)

            def norm_rows(l, n, buf, gain, bias, row_in, signal):
                alone(dve)
                for t in range(TT):
                    ins = v.bn_aggr(aggr[:, t, :], stats[:, t].rearrange("p h s -> p (h s)"))
                ins.then_inc(ln_var, 1)
                dve.wait_ge(ln_std, 3 * l + n + 1)
                then(l, v.reciprocal(rstd[:], std[:]))
                if gain is None:
                    for t in range(TT):
                        v.tensor_scalar(buf[:, t, :], buf[:, t, :], aggr[:, t, 0:1], rstd[:, t:t + 1],
                                        ALU.subtract, ALU.mult).then_inc(signal, 1)
                    return
                dve.wait_ge(rows_in, row_in)
                for t in range(TT):
                    then(l, v.tensor_scalar(buf[:, t, :], buf[:, t, :], aggr[:, t, 0:1], rstd[:, t:t + 1],
                                            ALU.subtract, ALU.mult))
                    then(l, v.tensor_tensor(buf[:, t, :], buf[:, t, :], gain, ALU.mult))
                    v.tensor_tensor(buf[:, t, :], buf[:, t, :], bias, ALU.add).then_inc(signal, 1)

            def residual(l, ps, gate, t, h):
                xs = x_tok[:, t, h * HALF:(h + 1) * HALF]
                v.tensor_tensor(tmp[:, 0, :], ps[:], gate_row[:, gate, h * HALF:(h + 1) * HALF], ALU.mult).then_inc(chain, 1)
                steps[0] += 1
                dve.wait_ge(chain, l * DVE_CHAIN + steps[0])
                then(l, v.scalar_tensor_tensor(out=xs, in0=xs, scalar=ALPHA, in1=tmp[:, 0, :],
                                               op0=ALU.mult, op1=ALU.add))
                return v.bn_stats(stats[:, t, h, :], xs)

            dve.wait_ge(c_ready, 1)
            for n in range(NEXT):
                dve.wait_ge(unit_in[n], 16)
                ada_sums(0, n, slot(n), lambda: dve.wait_ge(bank_full, n - 1) if n >= 2 else None, link_first)
                if n == 1:
                    dve.wait_ge(chan_in, 16)
                if n:
                    dve.wait_ge(bank_full, n)
                    drain(ada_store(0, n - 1, psum[n - 1]))
            dve.wait_ge(bank_full, NEXT)
            drain(ada_store(0, NEXT - 1, psum[NEXT - 1]))
            dve.wait_ge(drained["dve"], NEXT)
            dve.wait_ge(params_in, 16 * 6)
            with dve.Fori(0, DEPTH) as l:
                steps[0] = 0
                turn(l, "turn1", SHIFT1, SCALE1)
                for h in range(2):
                    dve.wait_ge(u_hi_ready, 2 * l + (h + 1))
                    k = slice(h * MT, (h + 1) * MT)
                    v.tensor_tensor(u_lo[:, k, :], u_ch[:, k, :], u_hi[:, k, :], ALU.subtract).then_inc(u_lo_ready, 1)

                def split(nth, lo, full, hi):
                    dve.wait_ge(y_hi_ready, 5 * l + (nth + 1))
                    v.tensor_tensor(lo, full, hi, ALU.subtract).then_inc(y_lo_ready, 1)

                ada_unit(l, 4)
                ada_unit(l, 5)
                dve.wait_ge(pads_ready, l + 1)
                for col in range(2):
                    after_drain(dve, l, ("in", 8 + col, 1))
                    for i in range(2):
                        what = ("in", 6 + col, i)
                        filled(dve, l, what)
                        k = MT * col + 2 * i
                        drain(v.tensor_tensor(cv_in[:, k:k + 2, CV_PAD:CV_PAD + T], ps2(what), flat(glu_sig, col, i), ALU.mult))
                    after_drain(dve, l, ("in", 6 + col, 1))
                    conv31(l, 2 * col, col)
                    if col == 0:
                        ada_out(l, 4)
                        ada_out(l, 5)

                after_drain(dve, l, ("in", 13, 1))
                for t in range(TT):
                    for h in range(2):
                        ins = v.bn_stats(stats[:, t, h, :], sg_v[:, t, h * HALF:(h + 1) * HALF])
                then(l, ins)
                norm_rows(l, 0, sg_v, sg_rows[:, 0, :], sg_rows[:, 1, :], 64 * l + 32, sgv_ready)
                dve.wait_ge(sgv_ready, TT * (l + 1))
                then(l, v.memset(sc_in[:, :, 0:SC_PAD], 0.0))
                for col in range(2):
                    after_drain(dve, l, ("in", 2 + col, 1))
                    for i in range(2):
                        what = ("in", 4 + col, i)
                        filled(dve, l, what)
                        k = MT * col + 2 * i
                        drain(v.tensor_tensor(sc_in[:, k:k + 2, SC_PAD:SC_PAD + T], ps2(what), flat(y_a, col, i), ALU.mult))
                    after_drain(dve, l, ("in", 4 + col, 1))
                    conv31(l, 2 * col + 1, 2 + col)
                    for i in range(2):
                        conv3(l, 2 * col + i)
                for col in range(2):
                    for i in range(2):
                        what = ("in", col, i)
                        filled(dve, l, what)
                        drain(v.tensor_tensor(flat(y_a, col, i), ps2(what), flat(y_a, col, i), ALU.mult))
                ada_unit(l, 6)
                after_drain(dve, l, ("in", 11, 1))
                for i in range(HEADS // 2):
                    what = ("mix", i)
                    filled(dve, l, what)
                    if i >= 2:
                        dve.wait_ge(yc_ready, (HEADS // 2) * l + i - 1)
                    srow = row_buf[:, 2, :].rearrange("p (h t) -> p h t", h=HEADS)
                    o4 = tmp[:, i % 2, :].rearrange("p (h n t) -> p h n t", h=2, n=TT)
                    drain(v.tensor_tensor(o4, bank(what)[:].rearrange("p (h n t) -> p h n t", h=2, n=TT),
                                          srow[:, 2 * i:2 * i + 2, :].unsqueeze(2).broadcast_to([P, 2, TT, P]), ALU.add))
                    after_drain(dve, l, what)
                    yc = y_c[:, 2 * i:2 * i + 2, :].rearrange("p k t -> p (k t)")
                    v.tensor_tensor(yc, yc, tmp[:, i % 2, :], ALU.mult).then_inc(yc_ready, 1)
                filled(dve, l, ("mean", 0))
                drain(v.tensor_tensor(y_b, y_b, bank(("mean", 0))[:, 0:T].unsqueeze(1).broadcast_to([P, KD, T]), ALU.subtract))
                ada_unit(l, 7)
                split(0, ya_lo[:], y_a, cv_hi[:])
                ada_out(l, 6)
                ada_out(l, 7)
                ada_unit(l, 8)
                after_drain(dve, l, ("var", 0))
                then(l, v.reciprocal(cv_rstd, cv_std))
                v.tensor_tensor(y_b, y_b, cv_rstd.unsqueeze(1).broadcast_to([P, KD, T]), ALU.mult).then_inc(cv_normed, 1)
                ada_unit(l, 9)

                def branch(b, gate, col, first=False):
                    after_drain(dve, l, ("gate", (b, col), 1))
                    for i in range(2):
                        what = ("branch", (b, col), i)
                        filled(dve, l, what)
                        if first:
                            drain(v.tensor_tensor(flat(merged, col, i), ps2(what), flat(gate, col, i), ALU.mult))
                        else:
                            t2 = tmp[:, i, :].rearrange("p (k t) -> p k t", k=2)
                            drain(v.tensor_tensor(t2, ps2(what), flat(gate, col, i), ALU.mult))
                            after_drain(dve, l, what)
                            ins = v.tensor_tensor(flat(merged, col, i), flat(merged, col, i), t2, ALU.add)
                            if b == 1:
                                ins.then_inc(merged_ready, 1)
                            else:
                                then(l, ins)

                branch(0, gate_a, 0, True)
                branch(0, gate_a, 1, True)
                split(1, yc_lo[:], y_c, cv_hi[:])
                split(2, yb_lo[:], y_b, yb_hi[:])
                ada_out(l, 8)
                ada_out(l, 9)
                after_drain(dve, l, ("ada", 9))
                then(l, v.tensor_tensor(fold[:], mod[:, SCALE2, :], chan_all(l, LN1_B), ALU.mult))
                then(l, v.tensor_tensor(mod[:, SHIFT2, :], mod[:, SHIFT2, :], fold[:], ALU.add))
                then(l, v.tensor_tensor(mod[:, SCALE2, :], mod[:, SCALE2, :], chan_all(l, LN1_G), ALU.mult))
                ada_unit(l, 10)
                ada_unit(l, 11)
                branch(2, gate_b, 0)
                ada_out(l, 10)
                ada_out(l, 11)
                ada_unit(l, 0)
                branch(2, gate_b, 1)
                ada_unit(l, 1)
                for col in range(2):
                    branch(1, gate_a, col)
                    k = slice(col * MT, (col + 1) * MT)
                    split(3 + col, merged_lo[:, k, :], merged[:, k, :], cv_hi[:, k, :])
                    if col == 0:
                        ada_out(l, 0)
                        ada_out(l, 1)
                        ada_unit(l, 2)
                ada_unit(l, 3)

                for h in range(2):
                    for t in range(TT):
                        filled(dve, l, ("o", h, t))
                        drain(residual(l, bank(("o", h, t)), 0, t, h))
                    if h == 0:
                        ada_out(l, 2)
                after_drain(dve, l, ("o", 1, 1))
                norm_rows(l, 1, x_tok, None, None, None, ln1_done)
                ada_out(l, 3)
                turn(l, "turn2", SHIFT2, SCALE2)

                def small(i):
                    return r_small[:, i]

                def groups(a):
                    return a.rearrange("p n (g e) -> p (n g) e", g=GROUPS)

                def over(ap, dim, shape):
                    return ap.unsqueeze(dim).broadcast_to(shape)

                LOG, EXP, SCORE, SEL, CHOSEN, CS, MASK, MS, G, PREF, DST, POS, W0 = range(13)
                partial = r_wide[:, 0]
                filled(dve, l, ("partial", 0))
                drain(v.tensor_copy(partial, bank(("partial", 0))[:, 0:T]))
                filled(dve, l, ("logits", 0))
                drain(v.tensor_copy(small(LOG), bank(("logits", 0))[:, 0:TT * EXPERTS].rearrange("p (n e) -> p n e", n=TT)))
                after_drain(dve, l, ("logits", 0))
                red = r_small[:, W0]
                then(l, v.tensor_reduce(red[:, 0, 0:TT], small(LOG), AX_X, ALU.max))
                v.tensor_tensor(small(LOG), small(LOG), over(red[:, 0, 0:TT], 2, [P, TT, EXPERTS]), ALU.subtract).then_inc(max_ready, 1)
                dve.wait_ge(exp_ready, l + 1)
                then(l, v.tensor_reduce(red[:, 0, 2:2 + TT], small(EXP), AX_X, ALU.add))
                then(l, v.reciprocal(red[:, 0, 4:4 + TT], red[:, 0, 2:2 + TT]))
                then(l, v.tensor_tensor(small(SCORE), small(EXP), over(red[:, 0, 4:4 + TT], 2, [P, TT, EXPERTS]), ALU.mult))
                then(l, v.tensor_tensor(small(SEL), small(SCORE), brout_sb[:].unsqueeze(1).broadcast_to([P, TT, EXPERTS]), ALU.add))
                dve.wait_ge(moe_consts_in, 32 * (l + 1))

                def beaten(src, rows_n, out_ap, gt, eq):
                    four = [P, rows_n, PER_GROUP, PER_GROUP]
                    other, own = src.unsqueeze(2).broadcast_to(four), src.unsqueeze(3).broadcast_to(four)
                    tri = tri16[:, 0:PER_GROUP, 0:PER_GROUP]
                    n = rows_n * PER_GROUP * PER_GROUP
                    g4 = r_wide[:, gt, 0:n].rearrange("p (r a b) -> p r a b", r=rows_n, a=PER_GROUP)
                    e4 = r_wide[:, eq, 0:n].rearrange("p (r a b) -> p r a b", r=rows_n, a=PER_GROUP)
                    v.tensor_tensor(g4, other, own, ALU.is_gt)
                    then(l, v.tensor_tensor(e4, other, own, ALU.is_equal))
                    then(l, v.tensor_tensor(e4, e4, tri.unsqueeze(1).broadcast_to(four), ALU.mult))
                    then(l, v.tensor_tensor(g4, g4, e4, ALU.add))
                    then(l, v.tensor_reduce(out_ap, g4, AX_X, ALU.add))

                rank = r_small[:, W0 + 1]
                beaten(groups(small(SEL)), TT * GROUPS, groups(rank), 0, 1)
                then(l, v.tensor_scalar(small(CHOSEN), rank, TOP_K - 0.5, None, ALU.is_lt))
                then(l, v.tensor_tensor(small(CS), small(CHOSEN), small(SEL), ALU.mult))
                gscore = red[:, 1, 0:TT * GROUPS]
                then(l, v.tensor_reduce(gscore, groups(small(CS)), AX_X, ALU.add))
                grank = red[:, 1, TT * GROUPS:2 * TT * GROUPS]
                beaten(gscore.rearrange("p (n g) -> p n g", n=TT), TT, grank.rearrange("p (n g) -> p n g", n=TT), 0, 1)
                then(l, v.tensor_scalar(grank, grank, 0.5, None, ALU.is_lt))
                then(l, v.tensor_tensor(groups(small(MASK)), groups(small(CHOSEN)),
                                        grank.unsqueeze(2).broadcast_to([P, TT * GROUPS, PER_GROUP]), ALU.mult))
                v.tensor_tensor(small(MS), small(MASK), small(SCORE), ALU.mult).then_inc(mask_ready, 1)
                dve.wait_ge(mask_ready, l + 1)
                then(l, v.tensor_reduce(red[:, 0, 6:6 + TT], small(MS), AX_X, ALU.add))
                then(l, v.reciprocal(red[:, 0, 8:8 + TT], red[:, 0, 6:6 + TT]))
                then(l, v.tensor_tensor(small(G), small(MS), over(red[:, 0, 8:8 + TT], 2, [P, TT, EXPERTS]), ALU.mult))
                filled(dve, l, ("ranks", 0))
                rk = bank(("ranks", 0))
                count = r_small[:, W0 + 2, 0]
                v.tensor_copy(small(PREF), rk[:, 0:TT * EXPERTS].rearrange("p (n e) -> p n e", n=TT))
                drain(v.tensor_copy(count, rk[:, TT * EXPERTS:(TT + 1) * EXPERTS]))
                after_drain(dve, l, ("ranks", 0))
                start = r_small[:, W0 + 2, 1]
                s16 = r_wide[:, 2].rearrange("p (a b) -> p a b", a=EXPERTS)
                then(l, v.tensor_tensor(s16, tri16, count.unsqueeze(1).broadcast_to([P, EXPERTS, EXPERTS]), ALU.mult))
                then(l, v.tensor_reduce(start, s16, AX_X, ALU.add))
                then(l, v.tensor_tensor(small(DST), small(PREF), start.unsqueeze(1).broadcast_to([P, TT, EXPERTS]), ALU.add))
                lo, hi = small(W0 + 3), small(W0 + 4)
                v.scalar_tensor_tensor(out=lo, in0=small(DST), scalar=-BIG, in1=small(MASK), op0=ALU.add, op1=ALU.mult)
                then(l, v.scalar_tensor_tensor(out=hi, in0=small(DST), scalar=1.0, in1=small(MASK), op0=ALU.add, op1=ALU.mult))
                v.tensor_reduce(red[:, 0, 10:10 + TT], lo, AX_X, ALU.min)
                then(l, v.tensor_reduce(red[:, 0, 12:12 + TT], hi, AX_X, ALU.max))
                then(l, v.tensor_scalar(red[:, 0, 12:12 + TT], red[:, 0, 12:12 + TT], -1.0, None, ALU.add))
                for t in range(TT):
                    ins = v.tensor_scalar(onehot[:, t, :], iota, red[:, 0, 10 + t:11 + t], BIG, ALU.subtract, ALU.is_equal)
                then(l, ins)
                for t in range(TT):
                    v.scalar_tensor_tensor(out=onehot[:, t, :], in0=iota, scalar=red[:, 0, 12 + t:13 + t], in1=onehot[:, t, :],
                                           op0=ALU.is_equal, op1=ALU.add).then_inc(onehot_ready, 1)
                nb = r_small[:, W0 + 5, 0]
                then(l, v.tensor_scalar(nb, count, float(BLOCK), 1.0, ALU.is_gt, ALU.add))
                for i in range(2, T // BLOCK):
                    then(l, v.scalar_tensor_tensor(out=nb, in0=count, scalar=float(i * BLOCK), in1=nb,
                                                   op0=ALU.is_gt, op1=ALU.add))
                v.tensor_copy(start_i[:], start[0:1, :])
                v.tensor_copy(blocks_i[:], nb[0:1, :]).then_inc(blocks_ready, 1)
                then(l, v.scalar_tensor_tensor(out=small(POS), in0=small(PREF), scalar=1.0, in1=small(MASK),
                                               op0=ALU.add, op1=ALU.mult))
                v.tensor_scalar(small(POS), small(POS), -1.0, None, ALU.add).then_inc(pos_step, 1)
                for k in range(1, KD, 2):
                    filled(dve, l, ("gather", k))
                    drain(v.tensor_scalar(sorted_ch[:, k, 0:SLOTS], bank(("gather", k))[:], mod[:, SCALE2, k:k + 1],
                                          mod[:, SHIFT2, k:k + 1], ALU.mult, ALU.add))
                after_drain(dve, l, ("gather", KD - 1))
                after_drain(dve, l, ("gather", KD - 2))
                dve.wait_ge(moe_zeroed, 4 * (l + 1))
                dve.wait_ge(blocks_ready, l + 1)
                alone(dve)

                def expert(pair, q):
                    e = 2 * pair + q
                    n = dve.value_load(blocks_i[0:1, bass.ds(e, 1)], min_val=1, max_val=T // BLOCK)
                    first = dve.value_load(start_i[0:1, bass.ds(e, 1)], min_val=0, max_val=SLOTS)
                    with dve.Fori(0, n) as i:
                        b = dve.snap(n_blk)
                        dve.wait_ge(h3_ready, b)
                        at_s = nc.s_assert_within(first + i * BLOCK, 0, SLOTS)
                        v.tensor_copy(xe, sorted_ch[:, :, bass.ds(at_s, BLOCK)]).then_inc(xe_ready, 1)
                        dve.wait_ge(turn_ready, b)
                        dve.wait_ge(pos_step, b + l)
                        other = pick[:, :, (1 - q) * BLOCK:(2 - q) * BLOCK]
                        if q == 0:
                            v.memset(other, 0.0)
                        else:
                            alone(dve)
                            with dve.If(i > 0):
                                v.memset(other, 0.0)
                        for t in range(TT):
                            pos_c = small(POS)[:, t, bass.ds(e, 1)]
                            g_c = small(G)[:, t, bass.ds(e, 1)]
                            ins = v.tensor_scalar(pick[:, t, q * BLOCK:(q + 1) * BLOCK], iota[:, 0:BLOCK],
                                                  pos_c, g_c, ALU.is_equal, ALU.mult)
                        ins.then_inc(pick_ready, 1)
                        dve.wait_ge(pick_ready, b + 1)
                        col = small(POS)[:, :, bass.ds(e, 1)]
                        v.tensor_scalar(col, col, -float(BLOCK), None, ALU.add).then_inc(pos_step, 1)
                        dve.wait_ge(silu_ready, b + 1)
                        dve.wait_ge(h3_ready, b + 1)
                        v.tensor_tensor(hid, ps_h3[:, 0:T], silu_e, ALU.mult).then_inc(hid_ready, 1)
                        dve.reg_add(n_blk, n_blk, 1)

                with dve.Fori(0, MOE_PAIRS) as pair:
                    for q in range(2):
                        expert(pair, q)

                dve.wait_ge(x_step, 2 * TT * (l + 1))
                for t in range(TT):
                    for h in range(2):
                        dve.wait_ge(moe_ready, 2 * TT * l + (2 * t + h + 1))
                        ins = residual(l, moe_sum[t][h], 1, t, h)
                then(l, ins)
                norm_rows(l, 2, x_tok, row_buf[:, 0, :], row_buf[:, 1, :], 64 * l + 64, ln2_done)
                assert steps[0] == DVE_CHAIN, steps[0]

        @block.tensor
        def _(pe):
            mm = nc.tensor.matmul
            n_blk = pe.alloc_register("pe_block")
            pe.reg_mov(n_blk, PRIMED)
            pe.sem_inc(h1_ready, PRIMED)
            pe.sem_inc(h3_ready, PRIMED)
            pe.sem_inc(turn_ready, PRIMED)
            pe.sem_inc(y_ready, PRIMED)

            def open_bank(l, what):
                i = USE[what]
                if i >= BANKS:
                    after_drain(pe, l, USES[i - BANKS][0])
                return psum[i % BANKS]

            def fill(what, ins):
                ins.then_inc(bank_full, 1)

            def ada(n, ps):
                acc = ada_sum[:, n % 2, :]
                if ADA_PARTS[n] in (2, 5):
                    ins = mm(ps[:], ones[:], acc, start=True, stop=True)
                else:
                    for m in range(MT):
                        ins = mm(ps[:, m:m + 1], acc[:, m * P:(m + 1) * P], ones[:, 0:1], start=True, stop=True)
                ins.then_inc(bank_full, 1)

            def product(l, unit, hi, lo, tokens_still=False, part_ready=None):
                u, m = UNIT[unit], PRODUCTS.index(unit)
                banks = [open_bank(l, (*unit, i)) for i in range(2)]
                wh, wl = w_hi[:, m % 2], w_lo[:, u % RAW]
                for c in range(CHUNKS):
                    if part_ready:
                        part_ready(c)
                    pe.wait_ge(w_lo_ready, l * (len(PRODUCTS) * CHUNKS) + (m * CHUNKS + c + 1))
                    for i in range(2):
                        for j in range(1 if tokens_still else 2):
                            for k in range(c * KC, (c + 1) * KC):
                                for n, (w, a) in enumerate(((wh, hi), (wh, lo), (wl, hi))):
                                    flags = dict(start=(k == 0 and n == 0 and j == 0), stop=(k == KD - 1 and n == 2), skip_group_check=True)
                                    if tokens_still:
                                        ins = mm(banks[i][:], a[:, k, i * P:(i + 1) * P], w[:, k, :], **flags)
                                    else:
                                        at_m = 2 * i + j
                                        ins = mm(banks[i][:, j * T:(j + 1) * T], w[:, k, at_m * P:(at_m + 1) * P], a[:, k, :], **flags)
                        if c == CHUNKS - 1:
                            fill((*unit, i), ins)
                    if c < CHUNKS - 1:
                        ins.then_inc(w_read, 1)

            def turn(l, name):
                for i in range(KD // 2):
                    ps = open_bank(l, (name, i))
                    for j in range(2):
                        for t in range(TT):
                            ins = nc.tensor.transpose(ps[:, j * T + t * P:j * T + (t + 1) * P],
                                                      x_tok[:, t, (2 * i + j) * P:(2 * i + j + 1) * P], ident[:])
                    fill((name, i), ins)
                after_drain(pe, l, (name, KD // 2 - 2))
                after_drain(pe, l, (name, KD // 2 - 1))

            def u_ready(l):
                def wait(c):
                    if c % (CHUNKS // 2) == 0:
                        pe.wait_ge(u_lo_ready, 2 * l + (c // (CHUNKS // 2) + 1))
                return wait

            def merged_split(l):
                def wait(c):
                    if c % (CHUNKS // 2) == 0:
                        pe.wait_ge(y_lo_ready, 5 * l + (c // (CHUNKS // 2) + 4))
                return wait

            pe.wait_ge(consts_ready, 4)
            for n in range(NEXT):
                pe.wait_ge(ada_ready, n + 1)
                ada(n, psum[n])
            pe.wait_ge(drained["dve"], NEXT)
            pe.wait_ge(params_in, 16 * 6)
            with pe.Fori(0, DEPTH) as l:
                pe.wait_ge(ln2_done, l * TT + PRIMED)
                turn(l, "turn1")
                for what, n in PE_ORDER:
                    if what == "mix":
                        pe.wait_ge(sgv_ready, TT * (l + 1))
                        pe.wait_ge(sgw_masked, l + 1)
                        for i in range(HEADS // 2):
                            ps = open_bank(l, ("mix", i))
                            for j in range(2):
                                h = 2 * i + j
                                for t in range(TT):
                                    ins = mm(ps[:, j * T + t * P:j * T + (t + 1) * P], sg_v[:, t, h * P:(h + 1) * P],
                                             sg_wm[:, h, :], start=True, stop=True)
                            fill(("mix", i), ins)
                    elif what in ("mean", "var"):
                        ps = open_bank(l, (what, 0))
                        if what == "mean":
                            pe.wait_ge(conv_step, (l + 1) * KD * CV_TAPS)
                        else:
                            pe.wait_ge(cv_squared, l + 1)
                        for k in range(KD):
                            ins = mm(ps[:, 0:T], mean_w[:], (y_b if what == "mean" else cv_sq)[:, k, :],
                                     start=(k == 0), stop=(k == KD - 1))
                        fill((what, 0), ins)
                    elif what == "ada":
                        ps = open_bank(l, (what, n))
                        ada_summed(pe, l, n)
                        ada(n, ps)
                    elif what == "in":
                        product(l, (what, n), u_hi, u_lo, tokens_still=n >= 12,
                                part_ready=u_ready(l) if n == 8 else None)
                    elif what == "gate":
                        product(l, (what, n), u_hi, u_lo)
                    elif what == "branch":
                        if n[1] == 0:
                            pe.wait_ge(y_lo_ready, 5 * l + {0: 1, 2: 2, 1: 3}[n[0]])
                        product(l, (what, n), yb_hi if n[0] == 1 else cv_hi, (ya_lo, yb_lo, yc_lo)[n[0]])
                    else:
                        product(l, (what, n), cv_hi, merged_lo, tokens_still=True, part_ready=merged_split(l) if n == 0 else None)
                pe.wait_ge(ln1_done, TT * (l + 1))
                turn(l, "turn2")
                ps = open_bank(l, ("partial", 0))
                for k in range(KD):
                    q = k % (P // QUAD)
                    ins = mm(ps[q * QUAD:(q + 1) * QUAD, 0:T], router_sb[:, k, :], u_ch[:, k, :],
                             start=(k < P // QUAD), stop=(k >= KD - P // QUAD), skip_group_check=True)
                fill(("partial", 0), ins)
                ps = open_bank(l, ("logits", 0))
                after_drain(pe, l, ("partial", 0))
                for t in range(TT):
                    ins = mm(ps[:, t * EXPERTS:(t + 1) * EXPERTS], r_wide[:, 0, t * P:(t + 1) * P], quad_sum[:],
                             start=True, stop=True)
                fill(("logits", 0), ins)
                ps = open_bank(l, ("ranks", 0))
                mask = r_small[:, 6]
                pe.wait_ge(mask_ready, l + 1)
                mm(ps[:, 0:EXPERTS], prec[:], mask[:, 0], start=True, stop=True)
                mm(ps[:, EXPERTS:2 * EXPERTS], ones[:], mask[:, 0], start=True, stop=False)
                mm(ps[:, EXPERTS:2 * EXPERTS], prec[:], mask[:, 1], start=False, stop=True)
                mm(ps[:, 2 * EXPERTS:3 * EXPERTS], ones[:], mask[:, 0], start=True, stop=False)
                fill(("ranks", 0), mm(ps[:, 2 * EXPERTS:3 * EXPERTS], ones[:], mask[:, 1], start=False, stop=True))
                for k in range(KD):
                    ps = open_bank(l, ("gather", k))
                    pe.wait_ge(onehot_ready, TT * (l + 1))
                    pe.wait_ge(x_lo_ready, TT * (l + 1))
                    for t in range(TT):
                        for n, part_x in enumerate((x_hi, x_lo)):
                            ins = mm(ps[:], part_x[:, t, k * P:(k + 1) * P], onehot[:, t, :],
                                     start=(t == 0 and n == 0), stop=(t == TT - 1 and n == 1))
                    fill(("gather", k), ins)

                pe.wait_ge(blocks_ready, l + 1)
                pe.wait_ge(moe_zeroed, 4 * (l + 1))
                after_drain(pe, l, ("gather", KD - 1))
                after_drain(pe, l, ("gather", KD - 2))
                for t in range(TT):
                    for h in range(2):
                        mm(moe_sum[t][h][:], turned[:, 0:P], y_two[:, h * HALF:(h + 1) * HALF], start=True, stop=False, skip_group_check=True)

                def combine(last=False):
                    for t in range(TT):
                        for h in range(2):
                            ins = mm(moe_sum[t][h][:], turned[:, 2 * P + t * P:2 * P + (t + 1) * P],
                                     y_two[:, h * HALF:(h + 1) * HALF], start=False, stop=last, skip_group_check=True)
                            if last:
                                ins.then_inc(moe_ready, 1)

                def expert(l, pair, q):
                    s0 = 3 * q
                    e = 2 * pair + q
                    for i in range(3):
                        s = s0 + i
                        pe.wait_ge(unit_in[s], 16 * (l * PER_SLOT[s] + pair + (MIX[s] + 1 + (s < NEXT))))
                    n = pe.value_load(blocks_i[0:1, bass.ds(e, 1)], min_val=1, max_val=T // BLOCK)
                    with pe.Fori(0, n) as i:
                        b = pe.snap(n_blk)
                        pe.wait_ge(xe_ready, b + 1)
                        for s, ps, ready in ((s0, ps_h1, h1_ready), (s0 + 1, ps_h3, h3_ready)):
                            w = slot(s)
                            for k in range(KD):
                                for h in range(2):
                                    ins = mm(ps[h * BLOCK:(h + 1) * BLOCK, 0:T], xe[:, k, :], w[:, k, h * T:(h + 1) * T],
                                             start=(k == 0), stop=(k == KD - 1))
                            ins.then_inc(ready, 1)
                        pe.wait_ge(y_copied, b)
                        if q == 0:
                            combine()
                        else:
                            with pe.If(i > 0):
                                combine()
                        pe.wait_ge(pick_ready, b + 1)
                        for t in range(TT):
                            nc.tensor.transpose(ps_turn[:, 2 * P + t * P:2 * P + (t + 1) * P],
                                                pick[:, t], ident[:])
                        pe.wait_ge(hid_ready, b + 1)
                        for c in range(2):
                            ins = nc.tensor.transpose(ps_turn[:, c * P:(c + 1) * P], hid[:, c * P:(c + 1) * P], ident[:])
                        ins.then_inc(turn_ready, 1)
                        pe.wait_ge(turned_ready, b + 1)
                        w = slot(s0 + 2, KE)
                        for f in range(KE):
                            half, c = f // 2, f % 2
                            for h in range(2):
                                ins = mm(ps_y[h * BLOCK:(h + 1) * BLOCK, :],
                                         turned[:, c * P + half * BLOCK:c * P + (half + 1) * BLOCK],
                                         w[:, f, h * HALF:(h + 1) * HALF], start=(f == 0), stop=(f == KE - 1))
                        ins.then_inc(y_ready, 1)
                        pe.reg_add(n_blk, n_blk, 1)

                with pe.Fori(0, MOE_PAIRS) as pair:
                    for q in range(2):
                        expert(l, pair, q)
                pe.wait_ge(y_copied, pe.snap(n_blk))
                combine(True)


def kernel(x, c, w_ada, b_ada, w_in, sc_conv, cv_conv, cv_conv_b, cv_ln_g, cv_ln_b, sg_ln_g, sg_ln_b,
           sg_w, sg_b, w_branch, w_gate, b_gate, w_o, ln1_g, ln1_b, w_router, b_router, w1, w3, w2,
           ln2_g, ln2_b):
    import numpy as np
    import concourse.bacc as bacc
    from concourse.bass_utils import run_bass_kernel_spmd

    def cols(a):
        return a.reshape(DEPTH, -1, KD, P).transpose(3, 0, 1, 2)

    ada = b_ada.reshape(DEPTH, 6, D)
    chan = np.concatenate([cols(ada[:, [0, 1, 3, 4]]), cols(sc_conv), cols(cv_conv), cols(cv_conv_b),
                           cols(cv_ln_g), cols(cv_ln_b), cols(b_gate), cols(ln1_g), cols(ln1_b)], axis=2)
    rows = np.stack([sg_ln_g, sg_ln_b, sg_b.reshape(DEPTH, D), ln1_g, ln1_b, ln2_g, ln2_b, ada[:, 2], ada[:, 5]], axis=1)
    i = np.arange(P)
    e = np.arange(EXPERTS)
    consts = np.zeros((P, N_CONST), np.float32)
    consts[:, C_ID:C_ID + P] = np.eye(P)
    consts[:, C_PREC:C_PREC + P] = i[:, None] < i[None, :]
    consts[:, C_TRI16:C_IOTA] = (e[None, :] < e[:, None]).reshape(1, -1)
    consts[:, C_FOLD:] = (i[:, None] % QUAD) == e[None, :]
    consts[:, C_IOTA:C_FOLD] = np.arange(SLOTS)[None, :]
    arrays = {
        "x": x.reshape(T, D), "c_cols": c.reshape(KD, P).T, "w_ada": w_ada, "w_in": w_in, "w_gate": w_gate,
        "w_branch": w_branch, "w_o": w_o, "w1": w1, "w3": w3, "w2": w2, "w_router": w_router,
        "b_router": b_router, "sg_wt": sg_w.transpose(0, 3, 1, 2), "chan": chan, "rows": rows, "consts": consts,
    }
    nc = bacc.Bacc("TRN2", target_bir_lowering=False, num_devices=1)
    feed, args = {}, []
    for name, a in arrays.items():
        a = np.ascontiguousarray(a)
        feed[f"in_{name}"] = a
        args.append(nc.dram_tensor(f"in_{name}", a.shape, mybir.dt.from_np(a.dtype), kind="ExternalInput").ap())
    args.append(nc.dram_tensor("out_x", (T, D), F32, kind="ExternalOutput").ap())
    build(nc, *args)
    result = run_bass_kernel_spmd(nc, [feed], core_ids=[0])
    return result.results[0]["out_x"].reshape(1, T, D)
```
